# Optimizing a Trainium2 kernel written in Bass

```python
import jax, jax.numpy as jnp
from jax import lax
import numpy as np

D_MODEL = 1024
BATCH = 1
SEQ = 256
DEPTH = 1

GRID_W = 64
CTX_LEN = 256
HGRN_HEADS = 4
HGRN_DK = 128
HGRN_DV = 128
HGRN_WIDTH = HGRN_HEADS * HGRN_DK
HGRN_CHUNK = 64
SGU_GROUPS = 4
SGU_CHUNK = 128
SGU_WIDTH = 512
SGU_GROUP_DIM = SGU_WIDTH // SGU_GROUPS
ROWS_PER_SGU_CHUNK = SGU_CHUNK // GRID_W
N_EXPERTS = 16
EXPERT_FF = 2048
CAPACITY_FACTOR = 2
N_MOD = 6
EPS = 1e-6
IN_COLS = 5 * HGRN_WIDTH + 2 * SGU_WIDTH + 2 * D_MODEL


def rmsnorm(x, w):
    xf = x.astype(jnp.float32)
    y = xf * lax.rsqrt(jnp.mean(xf * xf, axis=-1, keepdims=True) + EPS)
    return (y * w.astype(jnp.float32)).astype(x.dtype)

def adaln(cond, w, b):
    m = jax.nn.silu(cond) @ w + b
    m = m.reshape((-1, 1, N_MOD * D_MODEL))
    return jnp.split(m, N_MOD, axis=-1)

def modulate(h, shift, scale):
    return h * (1 + scale) + shift

def split_in(p):
    sizes = (HGRN_WIDTH,) * 5 + (SGU_WIDTH,) * 2 + (D_MODEL,) * 2
    idx = []
    acc = 0
    for s in sizes[:-1]:
        acc += s
        idx.append(acc)
    return jnp.split(p, idx, axis=-1)

def to_heads(a):
    return a.reshape(a.shape[0], a.shape[1], HGRN_HEADS, HGRN_DK)

def hgrn_forget(z, lb):
    f = lb + (1 - lb) * jax.nn.sigmoid(z.astype(jnp.float32))
    return jnp.log(f), 1 - f

def hgrn_chunk_scan(q, k, logf, v, s0):
    B_, T, H, DK = q.shape
    DV = v.shape[-1]
    nc = T // HGRN_CHUNK

    def to_chunks(a):
        return a.astype(jnp.float32).reshape(B_, nc, HGRN_CHUNK, H, a.shape[-1]).transpose(1, 0, 3, 2, 4)

    qc, kc, fc, vc = to_chunks(q), to_chunks(k), to_chunks(logf), to_chunks(v)
    mask = jnp.tril(jnp.ones((HGRN_CHUNK, HGRN_CHUNK), dtype=bool))[None, None, :, :, None]

    def step(S, inp):
        qb, kb, fb, vb = inp
        b = jnp.cumsum(fb, axis=2)
        diff = b[:, :, :, None, :] - b[:, :, None, :, :]
        decay = jnp.exp(jnp.where(mask, diff, -jnp.inf))
        scores = jnp.einsum('bhik,bhijk->bhij', qb, decay * kb[:, :, None, :, :])
        o = jnp.einsum('bhij,bhjv->bhiv', scores, vb) + jnp.einsum('bhik,bhkv->bhiv', qb * jnp.exp(b), S)
        b_last = b[:, :, -1:, :]
        S_new = jnp.exp(b_last[:, :, 0, :])[..., None] * S + jnp.einsum('bhjk,bhjv->bhkv', kb * jnp.exp(b_last - b), vb)
        return S_new, o

    s_fin, o = lax.scan(step, s0.astype(jnp.float32), (qc, kc, fc, vc))
    o = o.transpose(1, 0, 3, 2, 4).reshape(B_, T, H, DV)
    return o, s_fin

def hgrn_final_state(k, logf, v):
    b = jnp.cumsum(logf.astype(jnp.float32), axis=1)
    w = k.astype(jnp.float32) * jnp.exp(b[:, -1:] - b)
    return jnp.einsum('bthk,bthv->bhkv', w, v.astype(jnp.float32))

def sgu(u, v, norm_w, w_s, b_s, n_chunks):
    B_, T, _ = u.shape
    u = jax.nn.gelu(u).reshape(B_, n_chunks, SGU_CHUNK, SGU_GROUPS, SGU_GROUP_DIM)
    v = jax.nn.gelu(v).reshape(B_, T, SGU_GROUPS, SGU_GROUP_DIM)
    v = rmsnorm(v, norm_w.reshape(SGU_GROUPS, SGU_GROUP_DIM))
    v = v.reshape(B_, n_chunks, SGU_CHUNK, SGU_GROUPS, SGU_GROUP_DIM)
    mixed = jnp.einsum('gts,bnsgc->bntgc', w_s, v) + b_s.T[:, :, None]
    return (u * mixed).reshape(B_, T, SGU_WIDTH)

def token_mixer(parts, lb_f, lb_b, hgrn_norm_w, sgu_norm_w, sgu_w, sgu_b,
                w_branch_a, w_branch_b, w_out, s0_f, s0_b, n_sgu_chunks):
    q_p, ff_p, fb_p, v_p, g_p, u_p, sv_p, ga_p, gb_p = parts
    q = jax.nn.silu(to_heads(q_p))
    v = to_heads(v_p)
    logf_f, k_f = hgrn_forget(to_heads(ff_p), lb_f)
    logf_b, k_b = hgrn_forget(to_heads(fb_p), lb_b)
    o_f, s_f = hgrn_chunk_scan(q, k_f, logf_f, v, s0_f)
    o_b, s_b = hgrn_chunk_scan(q[:, ::-1], k_b[:, ::-1], logf_b[:, ::-1], v[:, ::-1], s0_b)
    o = o_f + o_b[:, ::-1]
    o = rmsnorm(o, hgrn_norm_w.reshape(HGRN_HEADS, HGRN_DV)).astype(g_p.dtype)
    o = o.reshape(o.shape[0], o.shape[1], HGRN_WIDTH) * jax.nn.silu(g_p)
    y_a = o @ w_branch_a
    y_b = sgu(u_p, sv_p, sgu_norm_w, sgu_w, sgu_b, n_sgu_chunks) @ w_branch_b
    merged = jax.nn.sigmoid(ga_p) * y_a + jax.nn.sigmoid(gb_p) * y_b
    return merged @ w_out, s_f, s_b

def moe_expert_choice(h, router_w, w_gate, w_up, w_down):
    B_, T, _ = h.shape
    cap = CAPACITY_FACTOR * T // N_EXPERTS
    aff = jax.nn.softmax((h @ router_w).astype(jnp.float32), axis=-1)
    gate, idx = lax.top_k(jnp.swapaxes(aff, 1, 2), cap)
    bidx = jnp.arange(B_)[:, None, None]
    xs = h[bidx, idx]
    hid = jax.nn.silu(jnp.einsum('becd,edf->becf', xs, w_gate)) * jnp.einsum('becd,edf->becf', xs, w_up)
    ye = jnp.einsum('becf,efd->becd', hid, w_down) * gate[..., None].astype(h.dtype)
    return jnp.zeros_like(h).at[bidx, idx].add(ye)

def first_inputs(seed: int = 0) -> dict:
    key = jax.random.key(seed)
    ks = jax.random.split(key, 24)
    f32 = jnp.float32
    nrm = lambda k, shape, s: jax.random.normal(k, shape, f32) * s
    return {
        'x': nrm(ks[0], (BATCH, SEQ, D_MODEL), 1.0),
        'c': nrm(ks[1], (BATCH, D_MODEL), 1.0),
        'ctx': nrm(ks[2], (BATCH, CTX_LEN, D_MODEL), 1.0),
        'c_ctx': nrm(ks[3], (D_MODEL,), 1.0),
        'ada_w': nrm(ks[4], (DEPTH, D_MODEL, N_MOD * D_MODEL), 0.02),
        'ada_b': nrm(ks[5], (DEPTH, N_MOD * D_MODEL), 0.02),
        'norm_mix_w': 1 + nrm(ks[6], (DEPTH, D_MODEL), 0.05),
        'norm_ffn_w': 1 + nrm(ks[7], (DEPTH, D_MODEL), 0.05),
        'w_in': nrm(ks[8], (DEPTH, D_MODEL, IN_COLS), D_MODEL ** -0.5),
        'hgrn_lb_logits': nrm(ks[9], (2, DEPTH + 1, HGRN_WIDTH), 0.5),
        'hgrn_norm_w': 1 + nrm(ks[10], (DEPTH, HGRN_WIDTH), 0.05),
        'sgu_norm_w': 1 + nrm(ks[11], (DEPTH, SGU_WIDTH), 0.05),
        'sgu_w': nrm(ks[12], (DEPTH, SGU_GROUPS, SGU_CHUNK, SGU_CHUNK), SGU_CHUNK ** -0.5),
        'sgu_b': 1 + nrm(ks[13], (DEPTH, SGU_GROUPS, SGU_CHUNK), 0.05),
        'w_branch_a': nrm(ks[14], (DEPTH, HGRN_WIDTH, D_MODEL), HGRN_WIDTH ** -0.5),
        'w_branch_b': nrm(ks[15], (DEPTH, SGU_WIDTH, D_MODEL), SGU_WIDTH ** -0.5),
        'w_out': nrm(ks[16], (DEPTH, D_MODEL, D_MODEL), D_MODEL ** -0.5),
        'router_w': nrm(ks[17], (DEPTH, D_MODEL, N_EXPERTS), D_MODEL ** -0.5),
        'expert_w_gate': nrm(ks[18], (DEPTH, N_EXPERTS, D_MODEL, EXPERT_FF), D_MODEL ** -0.5),
        'expert_w_up': nrm(ks[19], (DEPTH, N_EXPERTS, D_MODEL, EXPERT_FF), D_MODEL ** -0.5),
        'expert_w_down': nrm(ks[20], (DEPTH, N_EXPERTS, EXPERT_FF, D_MODEL), EXPERT_FF ** -0.5),
        'final_norm_w': 1 + nrm(ks[21], (D_MODEL,), 0.05),
    }

def first_block(x, c, ctx, c_ctx, ada_w, ada_b, norm_mix_w, norm_ffn_w, w_in, hgrn_lb_logits,
              hgrn_norm_w, sgu_norm_w, sgu_w, sgu_b, w_branch_a, w_branch_b, w_out, router_w,
              expert_w_gate, expert_w_up, expert_w_down, final_norm_w):
    B_, N, _ = x.shape
    ROWS = N // GRID_W
    n_sgu_lat = ROWS // ROWS_PER_SGU_CHUNK
    n_sgu_ctx = ctx.shape[1] // SGU_CHUNK
    lb_all = jnp.cumsum(jax.nn.softmax(hgrn_lb_logits.astype(jnp.float32), axis=1), axis=1)
    for l in range(DEPTH):
        last = l == DEPTH - 1
        lb_f = lb_all[0, l].reshape(HGRN_HEADS, HGRN_DK)
        lb_b = lb_all[1, l].reshape(HGRN_HEADS, HGRN_DK)
        sh_m, sc_m, g_m, sh_f, sc_f, g_f = adaln(c, ada_w[l], ada_b[l])
        csh_m, csc_m, cg_m, csh_f, csc_f, cg_f = adaln(c_ctx, ada_w[l], ada_b[l])

        h_ctx = modulate(rmsnorm(ctx, norm_mix_w[l]), csh_m, csc_m)
        pc = split_in(h_ctx @ w_in[l])
        if last:
            v_c = to_heads(pc[3])
            logf_f, k_f = hgrn_forget(to_heads(pc[1]), lb_f)
            logf_b, k_b = hgrn_forget(to_heads(pc[2]), lb_b)
            s_f = hgrn_final_state(k_f, logf_f, v_c)
            s_b = hgrn_final_state(k_b[:, ::-1], logf_b[:, ::-1], v_c[:, ::-1])
        else:
            zeros = jnp.zeros((ctx.shape[0], HGRN_HEADS, HGRN_DK, HGRN_DV), jnp.float32)
            y_c, s_f, s_b = token_mixer(pc, lb_f, lb_b, hgrn_norm_w[l], sgu_norm_w[l], sgu_w[l], sgu_b[l],
                                        w_branch_a[l], w_branch_b[l], w_out[l], zeros, zeros, n_sgu_ctx)
            ctx = ctx + cg_m * y_c
            h2c = modulate(rmsnorm(ctx, norm_ffn_w[l]), csh_f, csc_f)
            ctx = ctx + cg_f * moe_expert_choice(h2c, router_w[l], expert_w_gate[l], expert_w_up[l], expert_w_down[l])

        h = modulate(rmsnorm(x, norm_mix_w[l]), sh_m, sc_m)
        pl = split_in(h @ w_in[l])
        y, _, _ = token_mixer(pl, lb_f, lb_b, hgrn_norm_w[l], sgu_norm_w[l], sgu_w[l], sgu_b[l],
                              w_branch_a[l], w_branch_b[l], w_out[l], s_f, s_b, n_sgu_lat)
        x = x + g_m * y
        h2 = modulate(rmsnorm(x, norm_ffn_w[l]), sh_f, sc_f)
        x = x + g_f * moe_expert_choice(h2, router_w[l], expert_w_gate[l], expert_w_up[l], expert_w_down[l])
    return rmsnorm(x, final_norm_w)


GLA_HEADS = 4
GLA_DK = 128
GLA_DV = 256
GLA_KW = GLA_HEADS * GLA_DK
GLA_VW = GLA_HEADS * GLA_DV
GATE_RANK = 16
GATE_NORMALIZER = 16.0
GLA_CHUNK = 64
CONV_WIDTH = 1024
CONV_GROUPS = 8
CONV_K = 3
PLE_DIM = 256

SPLITS = [GLA_KW, GLA_KW, GLA_VW, GLA_VW, GATE_RANK,
          CONV_WIDTH, CONV_WIDTH, CONV_WIDTH, CONV_WIDTH,
          D_MODEL, D_MODEL]
IN_COLS_2 = sum(SPLITS)


def rms_norm(x, g):
    xf = x.astype(jnp.float32)
    y = xf * lax.rsqrt(jnp.mean(xf * xf, axis=-1, keepdims=True) + EPS)
    return (y * g.astype(jnp.float32)).astype(x.dtype)

def gla_chunked(q, k, v, gk):
    bsz, s, h, dk = q.shape
    dv = v.shape[-1]
    n = s // GLA_CHUNK

    def to_chunks(t):
        return t.astype(jnp.float32).reshape(bsz, n, GLA_CHUNK, h, t.shape[-1]).transpose(1, 0, 3, 2, 4)

    q, k, v, gk = to_chunks(q) * (dk ** -0.5), to_chunks(k), to_chunks(v), to_chunks(gk)
    b = jnp.cumsum(gk, axis=3)
    b_last = b[:, :, :, -1:, :]
    q_in = q * jnp.exp(b)
    k_in = k * jnp.exp(-b)
    k_dec = k * jnp.exp(b_last - b)
    causal = jnp.tril(jnp.ones((GLA_CHUNK, GLA_CHUNK), dtype=bool))
    a = jnp.where(causal, jnp.einsum('nbhid,nbhjd->nbhij', q_in, k_in), 0.0)
    o_intra = jnp.einsum('nbhij,nbhjv->nbhiv', a, v)
    decay = jnp.exp(b_last[:, :, :, 0, :])

    def step(state, xs):
        q_n, k_n, v_n, d_n = xs
        o_n = jnp.einsum('bhcd,bhdv->bhcv', q_n, state)
        state = d_n[..., None] * state + jnp.einsum('bhcd,bhcv->bhdv', k_n, v_n)
        return state, o_n

    state0 = jnp.zeros((bsz, h, dk, dv), jnp.float32)
    _, o_inter = lax.scan(step, state0, (q_in, k_dec, v, decay))
    o = o_intra + o_inter
    return o.transpose(1, 0, 3, 2, 4).reshape(bsz, s, h, dv)

def causal_dwconv(u, w):
    s = u.shape[1]
    u_pad = jnp.pad(u, ((0, 0), (CONV_K - 1, 0), (0, 0)))
    y = w[0] * u_pad[:, 0:s, :]
    for j in range(1, CONV_K):
        y = y + w[j] * u_pad[:, j:j + s, :]
    return y

def second_inputs(seed: int = 0) -> dict:
    key = jax.random.key(seed)
    ks = jax.random.split(key, 20)
    nrm = lambda k, shape, scale: jax.random.normal(k, shape, jnp.float32) * scale
    gain = lambda k, shape: 1.0 + 0.05 * jax.random.normal(k, shape, jnp.float32)
    return {
        "x": nrm(ks[0], (BATCH, SEQ, D_MODEL), 1.0),
        "p": nrm(ks[1], (DEPTH, BATCH, SEQ, PLE_DIM), 1.0),
        "norm_mix_g": gain(ks[2], (DEPTH, D_MODEL)),
        "w_in": nrm(ks[3], (DEPTH, D_MODEL, IN_COLS_2), D_MODEL ** -0.5),
        "b_merge": nrm(ks[4], (DEPTH, 2 * D_MODEL), 0.02),
        "w_gk2": nrm(ks[5], (DEPTH, GATE_RANK, GLA_KW), GATE_RANK ** -0.5),
        "b_gk": nrm(ks[6], (DEPTH, GLA_KW), 0.02),
        "gla_norm_g": gain(ks[7], (DEPTH, GLA_DV)),
        "conv_w": nrm(ks[8], (DEPTH, CONV_K, CONV_WIDTH), CONV_K ** -0.5),
        "w_branch_a": nrm(ks[9], (DEPTH, GLA_VW, D_MODEL), GLA_VW ** -0.5),
        "w_branch_c": nrm(ks[10], (DEPTH, CONV_WIDTH, D_MODEL), CONV_WIDTH ** -0.5),
        "w_out": nrm(ks[11], (DEPTH, D_MODEL, D_MODEL), D_MODEL ** -0.5),
        "norm_ple_g": gain(ks[12], (DEPTH, D_MODEL)),
        "w_ple_gate": nrm(ks[13], (DEPTH, D_MODEL, D_MODEL), D_MODEL ** -0.5),
        "w_ple_proj": nrm(ks[14], (DEPTH, PLE_DIM, D_MODEL), PLE_DIM ** -0.5),
        "norm_final_g": gain(ks[15], (D_MODEL,)),
    }

def second_block(x, p, norm_mix_g, w_in, b_merge, w_gk2, b_gk, gla_norm_g, conv_w,
              w_branch_a, w_branch_c, w_out, norm_ple_g, w_ple_gate, w_ple_proj,
              norm_final_g):
    bsz, s, _ = x.shape
    idx = np.cumsum(SPLITS)[:-1].tolist()
    for i in range(DEPTH):
        h = rms_norm(x, norm_mix_g[i])
        proj = jnp.einsum('bsd,dc->bsc', h, w_in[i])
        (q, k, v, z_a, gk_low, cb, cc, xc, z_c, g_a, g_c) = jnp.split(proj, idx, axis=-1)

        gk = jax.nn.log_sigmoid((jnp.einsum('bsr,rk->bsk', gk_low, w_gk2[i]) + b_gk[i]).astype(jnp.float32)) / GATE_NORMALIZER
        o = gla_chunked(q.reshape(bsz, s, GLA_HEADS, GLA_DK),
                        k.reshape(bsz, s, GLA_HEADS, GLA_DK),
                        v.reshape(bsz, s, GLA_HEADS, GLA_DV),
                        gk.reshape(bsz, s, GLA_HEADS, GLA_DK))
        o = rms_norm(o, gla_norm_g[i]).reshape(bsz, s, GLA_VW).astype(x.dtype)
        y_a = jnp.einsum('bsv,vd->bsd', o * jax.nn.silu(z_a), w_branch_a[i])

        u = causal_dwconv(cc * xc, conv_w[i])
        y_c = jnp.einsum('bsc,cd->bsd', (cb * u) * jax.nn.silu(z_c), w_branch_c[i])

        b_ga, b_gc = b_merge[i][:D_MODEL], b_merge[i][D_MODEL:]
        merged = jax.nn.sigmoid(g_a + b_ga) * y_a + jax.nn.sigmoid(g_c + b_gc) * y_c
        x = x + jnp.einsum('bsd,de->bse', merged, w_out[i])

        ple_gate = jax.nn.sigmoid(jnp.einsum('bsd,de->bse', rms_norm(x, norm_ple_g[i]), w_ple_gate[i]))
        x = x + ple_gate * jnp.einsum('bsq,qd->bsd', p[i], w_ple_proj[i])
    return rms_norm(x, norm_final_g)


def setup_inputs(seed=0):
    out = dict(first_inputs(seed))
    for name, value in second_inputs(seed + 1).items():
        if name != "x":
            out[name + "_2"] = value
    return out


def reference(
    x, c, ctx, c_ctx, ada_w, ada_b, norm_mix_w, norm_ffn_w, w_in, hgrn_lb_logits, hgrn_norm_w,
    sgu_norm_w, sgu_w, sgu_b, w_branch_a, w_branch_b, w_out, router_w, expert_w_gate,
    expert_w_up, expert_w_down, final_norm_w, p_2, norm_mix_g_2, w_in_2, b_merge_2, w_gk2_2,
    b_gk_2, gla_norm_g_2, conv_w_2, w_branch_a_2, w_branch_c_2, w_out_2, norm_ple_g_2,
    w_ple_gate_2, w_ple_proj_2, norm_final_g_2,
):
    x = first_block(
        x, c, ctx, c_ctx, ada_w, ada_b, norm_mix_w, norm_ffn_w, w_in, hgrn_lb_logits,
        hgrn_norm_w, sgu_norm_w, sgu_w, sgu_b, w_branch_a, w_branch_b, w_out, router_w,
        expert_w_gate, expert_w_up, expert_w_down, final_norm_w,
    )
    return second_block(
        x, p_2, norm_mix_g_2, w_in_2, b_merge_2, w_gk2_2, b_gk_2, gla_norm_g_2, conv_w_2,
        w_branch_a_2, w_branch_c_2, w_out_2, norm_ple_g_2, w_ple_gate_2, w_ple_proj_2,
        norm_final_g_2,
    )


_drawn_inputs = setup_inputs


def setup_inputs(seed=0):
    import zlib

    import numpy as np

    out = dict(_drawn_inputs(seed))
    spreads = {}
    factors = {'ctx': 7.957,
     'c_ctx': 7.812,
     'norm_ffn_w': 3.087,
     'hgrn_lb_logits': 6.969,
     'hgrn_norm_w': 5.081,
     'sgu_norm_w': 5.005,
     'sgu_b': 5.274,
     'b_merge_2': 8.0,
     'b_gk_2': 8.0,
     'gla_norm_g_2': 4.485,
     'norm_ple_g_2': 22.341}
    for name, (base, spread) in spreads.items():
        noise = np.random.default_rng([zlib.crc32(name.encode()), seed]).standard_normal(out[name].shape)
        drawn = base * np.exp(spread * noise) if base else spread * noise
        out[name] = __import__('jax').numpy.asarray(drawn.astype(out[name].dtype))
    for name, factor in factors.items():
        out[name] = (out[name] * factor).astype(out[name].dtype)
    return out
```

```python
from contextlib import ExitStack

import numpy as np

import concourse.bass as bass
from concourse import mybir

F32 = mybir.dt.float32
U8 = mybir.dt.uint8
ALU = mybir.AluOpType
ACT = mybir.ActivationFunctionType
AX = mybir.AxisListType.X

T = 256
D = 1024
NE = 16
CAP = 32
FF = 2048
EPS = 1e-6
SLOT = 2048
BASE_SLOTS = 8
MORE_SLOTS = 8
GELU_C = 2.0 * 0.7978845608028654

VEC = dict(c=16, ada_b=48, nmix=8, nffn=8, lb=16, hgn=4, sgn=4, fnw=8, nm2=8, bm2=16, bgk=4, gng=2,
           cw=24, nple=8, nfin=8, eps=1)
VOFF, VN = {}, 0
for _k, _n in VEC.items():
    VOFF[_k] = VN
    VN += _n


class Queue:

    def __init__(self, sem, linked):
        self.sem, self.linked, self.n, self.ops, self.seen = sem, linked, 0, [], {}
        self.value = {}

    def __call__(self, fn, *waits, link=True):
        waits = list(waits)
        if self.linked and link and self.n:
            waits.append((self, self.n))
        self.ops.append((news(self.seen, waits), fn))
        self.n += 1
        return (self, self.n)

    def last(self):
        return (self, self.n)

    def emit(self, eng):
        for n, (need, fn) in enumerate(self.ops):
            for w in need:
                await_(eng, w)
            ins = fn(eng)
            if n + 1 in self.value:
                ins.then_inc(self.sem, 1)


def news(seen, waits):
    need = []
    for w in flat(waits):
        if seen.get(id(w[0]), 0) < w[1]:
            seen[id(w[0])] = w[1]
            need.append(w)
    return need


def await_(eng, w):
    src, n = w
    if isinstance(src, Queue):
        eng.wait_ge(src.sem, src.value[n])
    else:
        eng.wait_ge(src, n)


def number(queues, needs):
    used = {}
    for src, n in needs + [w for q in queues for need, _ in q.ops for w in need]:
        if isinstance(src, Queue):
            used.setdefault(id(src), set()).add(n)
    for q in queues:
        q.value = {n: i + 1 for i, n in enumerate(sorted(used.get(id(q), ())))}


def flat(x):
    if x is None:
        return []
    if isinstance(x, list):
        return [z for y in x for z in flat(y)]
    return [x]


def program(nc, a, out):
    ctx = ExitStack()
    with ctx:
        def sem(name):
            return ctx.enter_context(nc.semaphore(name))

        TOT = 52992
        M = ctx.enter_context(nc.sbuf_tensor("M", [128, TOT], F32))
        B = [ctx.enter_context(nc.psum_tensor(f"B{i}", [128, 512], F32))[:, :] for i in range(8)]

        PE = Queue(sem("s_pe"), False)
        V = Queue(sem("s_dve"), True)
        A = Queue(sem("s_act"), True)
        G = Queue(sem("s_pool"), True)
        SP = []

        pos = [0]

        def new(n, at=None):
            o = pos[0] if at is None else at[0]
            (pos if at is None else at)[0] = o + n
            assert o + n <= TOT, (o, n)
            return M[:, o:o + n]

        slots = [new(SLOT) for _ in range(BASE_SLOTS)]
        XX = new(2048).rearrange("p (k t) -> p k t", k=8)
        vec = new(VN)
        ones = new(128)
        ident = new(128)
        iot = new(32)
        cms = new(288)
        msk = cms.bitcast(U8).rearrange("p (s i) -> p s i", s=9)
        csil = new(256).rearrange("p (k r) -> p k r", k=8)
        mod = new(96).rearrange("p (m r) -> p m r", r=2)
        swm = new(16).rearrange("p (k r) -> p k r", r=2)
        swf = new(8)
        lbv = new(32)
        ctmp = new(64)
        wr = new(128).rearrange("p (k n) -> p k n", k=8)
        zone = pos[0]
        z1 = [zone]
        more = [new(SLOT, z1) for _ in range(MORE_SLOTS)]
        late = z1[0]
        z1 = [zone]
        XC = new(2048, z1).rearrange("p (k t) -> p k t", k=8)
        HT = new(4096, z1).rearrange("p (k t) -> p k t", k=8)
        vx = new(1024, z1).rearrange("p (i n) -> p i n", i=2)
        vc = new(1024, z1).rearrange("p (i n) -> p i n", i=2)
        wtok = new(2048, z1).rearrange("p (i n) -> p i n", i=2)
        St = new(1024, z1).rearrange("p (d n) -> p d n", d=2)
        PT = new(2048, z1).rearrange("p (j h i) -> p j h i", j=2, h=4)
        bf = new(1024, z1).rearrange("p (h t) -> p h t", h=4)
        bb = new(1024, z1).rearrange("p (h t) -> p h t", h=4)
        kf = new(1024, z1).rearrange("p (h t) -> p h t", h=4)
        kb = new(1024, z1).rearrange("p (h t) -> p h t", h=4)
        qT = new(1024, z1).rearrange("p (h t) -> p h t", h=4)
        EK = new(1024, z1).rearrange("p (h t) -> p h t", h=4)
        EQ = new(1024, z1).rearrange("p (h t) -> p h t", h=4)
        MK = new(1024, z1).rearrange("p (h t) -> p h t", h=4)
        MQ = new(1024, z1).rearrange("p (h t) -> p h t", h=4)
        oT = kf
        gT = new(1024, z1).rearrange("p (h t) -> p h t", h=4)
        uT = new(1024, z1).rearrange("p (h t) -> p h t", h=4)
        svt = new(1024, z1).rearrange("p (i n) -> p i n", i=2)
        tmp = [new(512, z1) for _ in range(6)]
        wst = new(512, z1).rearrange("p (g t) -> p g t", g=4)
        bsb = new(512, z1).rearrange("p (g t) -> p g t", g=4)
        wctx, SA = XC, XC
        SB = wtok.rearrange("p i n -> p (i n)").rearrange("p (k t) -> p k t", k=8)
        MG = HT[:, :, 0:256]

        def vc_(name, i=0, n=1):
            return vec[:, VOFF[name] + i:VOFF[name] + i + n]

        def load(dst, src, name):
            s = sem(name)
            early.append((dst, src, s))
            return (s, 16)

        early = []
        t_vec = load(vec, a["vec"], "l_vec")
        t_x = load(XX, a["x"].rearrange("(k p) t -> p k t", p=128), "l_x")
        t_c = load(XC, a["ctx"].rearrange("(k p) t -> p k t", p=128), "l_c")
        t_mf = load(PT.rearrange("p j h i -> p (j h i)")[:, 0:1152], a["msk"], "l_msk")
        t_id = load(ident, a["ident"], "l_id")
        t_iot = load(iot, a["iota"], "l_iot")
        t_wst = load(wst, a["wst"].rearrange("g s t -> s g t"), "l_wst")
        t_bsb = load(bsb, a["sgu_b"].rearrange("(o g) t -> o (g t)", o=1).broadcast_to([128, 512]), "l_bsb")
        t_wr = load(wr, a["router_w"].rearrange("(k p) n -> p k n", p=128), "l_wr")

        freed = {}
        ring = list(range(BASE_SLOTS))
        at = [0]
        ssem = [sem(f"r{i}") for i in range(BASE_SLOTS + MORE_SLOTS)]
        scount = [0] * (BASE_SLOTS + MORE_SLOTS)
        allslots = slots + more
        last_done = {}

        class Slot:
            pass

        items = []

        def stream(src, shape, parts=128):
            i = ring[at[0] % len(ring)]
            at[0] += 1
            s = Slot()
            s.i = i
            n = int(np.prod(shape))
            view = allslots[i][0:parts, 0:n]
            if len(shape) == 2:
                view = view.rearrange("p (a b) -> p a b", a=shape[0])
            elif len(shape) == 3:
                view = view.rearrange("p (a b c) -> p a b c", a=shape[0], b=shape[1])
            s.v = view
            scount[i] += 16
            s.t = (ssem[i], scount[i])
            s.prev = last_done.get(i)
            last_done[i] = s
            s.free = None
            SP.append((s, view, src))
            return s

        def done(s, tok):
            s.free = tok

        def finish(final):
            outs = []
            everything = [q.last() for q in (PE, V, A, G) if q.n] + [(s, 16) for _, _, s in early]
            outs.append((out.rearrange("(k p) t -> p k t", p=128), final))
            s_out = sem("s_out")
            block = ctx.enter_context(nc.Block())

            seen, loads = {}, []
            for sl_, view, src in SP:
                need = news(seen, sl_.prev.free if sl_.prev is not None else None)
                loads.append((need, view, src, ssem[sl_.i]))
            number([PE, V, A, G], [w for need, *_ in loads for w in need] + everything)

            @block.sync
            def _(eng):
                for need, view, src, s in loads:
                    for w in need:
                        await_(eng, w)
                    eng.dma_start(view, src).then_inc(s, 16)
                for w in everything:
                    await_(eng, w)
                for dst, src in outs:
                    eng.dma_start(dst, src).then_inc(s_out, 16)
                eng.wait_ge(s_out, 16 * len(outs))

            @block.scalar
            def _(eng):
                for dst, src, s in early:
                    eng.dma_start(dst, src).then_inc(s, 16)
                eng.preload_act_table_set("natural_log_exp_and_others")
                A.emit(eng)

            @block.vector
            def _(eng):
                V.emit(eng)

            @block.gpsimd
            def _(eng):
                G.emit(eng)

            @block.tensor
            def _(eng):
                PE.emit(eng)

        g0 = G(lambda e: e.memset(ones, 1.0))
        t_msk = G(lambda e: e.tensor_copy(cms.bitcast(U8), PT.rearrange("p j h i -> p (j h i)")[:, 0:1152]), t_mf)
        g1 = G(lambda e: e.memset(csil.rearrange("p k r -> p (k r)"), 0.0))
        cv = vc_("c", 0, 16)
        a0 = A(lambda e: e.activation(ctmp[:, 0:16], cv, ACT.Exp, scale=-1.0), t_vec)
        V(lambda e: e.tensor_scalar(ctmp[:, 16:32], ctmp[:, 0:16], 1.0, None, ALU.add), a0)
        V(lambda e: e.reciprocal(ctmp[:, 32:48], ctmp[:, 16:32]))
        t_csil = V(lambda e: e.tensor_tensor(csil[:, :, 0:2], cv.rearrange("p (k r) -> p k r", r=2),
                                             ctmp[:, 32:48].rearrange("p (k r) -> p k r", r=2), ALU.mult),
                   t_vec, g1)
        lg = vc_("lb", 0, 16).rearrange("p (d l h) -> p d l h", d=2, l=2)
        lt = ctmp[:, 0:16].rearrange("p (d l h) -> p d l h", d=2, l=2)
        mx = ctmp[:, 16:24].rearrange("p (d h) -> p d h", d=2)
        V(lambda e: e.tensor_tensor(mx, lg[:, :, 0, :], lg[:, :, 1, :], ALU.max))
        V(lambda e: e.tensor_tensor(lt[:, :, 0, :], lg[:, :, 0, :], mx, ALU.subtract))
        v0 = V(lambda e: e.tensor_tensor(lt[:, :, 1, :], lg[:, :, 1, :], mx, ALU.subtract))
        a1 = A(lambda e: e.activation(ctmp[:, 24:40], ctmp[:, 0:16], ACT.Exp), v0)
        le = ctmp[:, 24:40].rearrange("p (d l h) -> p d l h", d=2, l=2)
        V(lambda e: e.tensor_tensor(mx, le[:, :, 0, :], le[:, :, 1, :], ALU.add), a1)
        V(lambda e: e.reciprocal(ctmp[:, 40:48], ctmp[:, 16:24]))
        V(lambda e: e.tensor_tensor(lbv[:, 0:8].rearrange("p (d h) -> p d h", d=2), le[:, :, 0, :],
                                    ctmp[:, 40:48].rearrange("p (d h) -> p d h", d=2), ALU.mult))
        t_lb = V(lambda e: e.tensor_scalar(lbv[:, 8:16], lbv[:, 0:8], -1.0, 1.0, ALU.mult, ALU.add))
        lb = lambda d, h: lbv[:, 4 * d + h:4 * d + h + 1]
        olb = lambda d, h: lbv[:, 8 + 4 * d + h:9 + 4 * d + h]

        def rstd(dst, src, n, *waits):
            t = A(lambda e: e.activation(dst, src, ACT.Ln, bias=vc_("eps"), scale=1.0 / n), *waits)
            return A(lambda e: e.activation(dst, dst, ACT.Exp, scale=-0.5))

        free = {i: None for i in range(8)}

        SQ = [EK, EQ, MK, MQ]
        rs = tmp[0]
        s_all = []
        for which, (src, tsrc) in enumerate(((XC, t_c), (XX, t_x))):
            part = tmp[1][:, 256 * which:256 * which + 256]
            toks = []
            for h in range(2):
                sq = SQ[2 * which + h]
                toks.append(A(lambda e, sq=sq, src=src, h=h: e.activation(sq, src[:, 4 * h:4 * h + 4, :], ACT.Square), tsrc))
            lo, hi = SQ[2 * which], SQ[2 * which + 1]
            V(lambda e, lo=lo, hi=hi: e.tensor_tensor(lo, lo, hi, ALU.add), toks)
            V(lambda e, lo=lo: e.tensor_tensor(lo[:, 0:2, :], lo[:, 0:2, :], lo[:, 2:4, :], ALU.add))
            s_all.append(V(lambda e, lo=lo, part=part: e.tensor_tensor(part, lo[:, 0, :], lo[:, 1, :], ALU.add)))
        p0 = PE(lambda e: e.matmul(B[0], ones, tmp[1], start=True, stop=True), s_all, g0)
        t_rs = free[0] = rstd(rs, B[0], D, p0)
        for k in range(8):
            V(lambda e, k=k: e.tensor_tensor(HT[:, k, 0:256], XC[:, k, :], rs[:, 0:256], ALU.mult), t_rs)
            t_xn = V(lambda e, k=k: e.tensor_tensor(HT[:, k, 256:512], XX[:, k, :], rs[:, 256:512], ALU.mult))

        def ada(q):
            bank = B[0]
            sl = [stream(a["ada_w"][k * 128:(k + 1) * 128, q * 2048:(q + 1) * 2048], [2048]) for k in range(8)]
            for k in range(8):
                for j in range(4):
                    tok = PE(lambda e, k=k, j=j: e.matmul(bank[32 * j:32 * j + 32, :], csil[:, k, :],
                                                          sl[k].v[:, 512 * j:512 * j + 512],
                                                          start=k == 0, stop=k == 7),
                             sl[k].t, t_csil, free[0])
                done(sl[k], tok)
            row = tmp[2]
            vt = V(lambda e: e.tensor_copy(row, bank[:, :]), tok)
            free[0] = vt
            for c in range(4):
                tok = PE(lambda e, c=c: e.transpose(B[1][:, 128 * c:128 * c + 128], row[:, 128 * c:128 * c + 128], ident),
                         vt, t_id, free[1])
            o = mod[:, 16 * q:16 * q + 16, :].rearrange("p (j c) r -> p j c r", j=4)
            i0 = B[1][:, :].rearrange("p (c j r) -> p j c r", c=4, j=4)
            bias = vc_("ada_b", 16 * q, 16).rearrange("p (j c o) -> p j c o", j=4, o=1).broadcast_to([128, 4, 4, 2])
            for r in range(2):
                free[1] = V(lambda e, r=r: e.tensor_tensor(o[:, :, :, r], i0[:, :, :, r], bias[:, :, :, r], ALU.add), tok)
            return free[1]

        t_a0 = ada(0)
        nb = vc_("nmix", 0, 8).rearrange("p (k o) -> p k o", o=1).broadcast_to([128, 8, 2])
        for r in range(2):
            t_sw = V(lambda e, r=r: e.scalar_tensor_tensor(swm[:, :, r], mod[:, 8:16, r], 1.0, nb[:, :, r],
                                                           ALU.add, ALU.mult))
        hts = []
        for k in range(8):
            for r, cols in ((1, slice(0, 256)), (0, slice(256, 512))):
                hv = HT[:, k, cols]
                f = lambda e, k=k, r=r, hv=hv: e.tensor_scalar(hv, hv, swm[:, k, r:r + 1], mod[:, k, r:r + 1], ALU.mult, ALU.add)
                g = lambda e, k=k, r=r, hv=hv: e.activation(hv, hv, ACT.Identity, bias=mod[:, k, r:r + 1], scale=swm[:, k, r:r + 1])
                hts.append(V(f) if r else A(g, t_sw, t_xn))
        t_h = [hts[-1], hts[-2]]

        bankno = [0]

        def nextbank():
            bankno[0] ^= 1
            return 2 + bankno[0]

        def projT(W, slots_, cols, rhs, n, bank, waits, kn=8):
            for k in range(kn):
                tok = PE(lambda e, k=k: e.matmul(bank, W[:, k, cols], rhs(k), start=k == 0, stop=k == kn - 1),
                         *(waits if k == 0 else []))
            return tok

        QO, FO, BO, VO, GO, UO, SO, AO, CO = 0, 512, 1024, 1536, 2048, 2560, 3072, 3584, 4608
        win = a["w_in"].rearrange("(k p) n -> p k n", p=128)

        def wslot(src, c0, n=256, kn=8):
            return stream(src[:, :, c0:c0 + n], [kn, n])

        Hx = lambda k: HT[:, k, 256:512]
        Hall = lambda k: HT[:, k, :]

        def sigmoid(dst, src, *waits):
            w = V(lambda e: e.tensor_scalar(dst, src, -43.0, None, ALU.max), *waits)
            A(lambda e: e.activation(dst, dst, ACT.Exp, scale=-1.0), w)
            A(lambda e: e.activation(dst, dst, ACT.Ln, bias=ones[:, 0:1]))
            return A(lambda e: e.activation(dst, dst, ACT.Exp, scale=-1.0)), w

        tk = {}
        for d in range(2):
            for hh in range(2):
                s = wslot(win, (FO, BO)[d] + 256 * hh)
                for j in range(2):
                    h = 2 * hh + j
                    b = nextbank()
                    ps = B[b]
                    tok = projT(s.v, s, slice(128 * j, 128 * j + 128), Hall, 512, ps[:, :], [s.t, t_h, free[b]])
                    if j:
                        done(s, tok)
                    f, lf, cu = tmp[(h % 2) * 3], tmp[(h % 2) * 3 + 1], tmp[(h % 2) * 3 + 2]
                    t0, free[b] = sigmoid(f, ps[:, :], tok, tk.get(("f", h % 2)))
                    V(lambda e, f=f, d=d, h=h: e.tensor_scalar(f, f, olb(d, h), lb(d, h), ALU.mult, ALU.add), t0)
                    t1 = V.last()
                    ta = A(lambda e, f=f, lf=lf: e.activation(lf, f, ACT.Ln), t1)
                    kx, bx = (kf, kb)[d], (bf, bb)[d]
                    V(lambda e, f=f, kx=kx, h=h: e.tensor_scalar(kx[:, h, :], f[:, 256:512], -1.0, 1.0, ALU.mult, ALU.add))
                    kc = cu[:, 256:512]
                    V(lambda e, f=f, kc=kc: e.tensor_scalar(kc, f[:, 0:256], -1.0, 1.0, ALU.mult, ALU.add))
                    st = -1 if d else 1
                    onr = ones[:, 0:1].broadcast_to([128, 256])
                    V(lambda e, bx=bx, h=h, lf=lf, st=st, onr=onr: e.tensor_tensor_scan(
                        bx[:, h, ::st], onr, lf[:, 256:512][:, ::st], 0.0, ALU.mult, ALU.add), ta, g0)
                    cc = cu[:, 0:256]
                    t2 = V(lambda e, cc=cc, lf=lf, st=st, onr=onr: e.tensor_tensor_scan(
                        cc[:, ::st], onr, lf[:, 0:256][:, ::st], 0.0, ALU.mult, ALU.add))
                    lastc = cc[:, 0:1] if d else cc[:, 255:256]
                    t3 = A(lambda e, f=f, cc=cc, lastc=lastc: e.activation(f[:, 0:256], cc, ACT.Exp, bias=lastc, scale=-1.0), t2)
                    tk["f", h % 2] = t3
                    tw = V(lambda e, f=f, kc=kc, d=d, h=h: e.tensor_tensor(wctx[:, 4 * d + h, :], kc, f[:, 0:256], ALU.mult), t3)
                    tk["w", d, h] = tw
                    tk["f", h % 2] = [t3, tw]
            tk["b", d] = tw

        for hh in range(2):
            s = wslot(win, VO + 256 * hh)
            for i in range(4):
                b = nextbank()
                for k in range(8):
                    tok = PE(lambda e, k=k, b=b, s=s, i=i: e.matmul(B[b][:, 0:256], HT[:, k, 128 * i:128 * i + 128], s.v[:, k, :],
                                                                    start=k == 0, stop=k == 7), s.t, free[b])
                dst = (vc, vx)[i // 2][:, i % 2, 256 * hh:256 * hh + 256]
                free[b] = A(lambda e, dst=dst, b=b: e.activation(dst, B[b][:, 0:256], ACT.Copy), tok)
            done(s, tok)
        t_v = free[b]

        for hh in range(2):
            s = wslot(win, QO + 256 * hh)
            b = nextbank()
            for j in range(2):
                tok = projT(s.v, s, slice(128 * j, 128 * j + 128), Hx, 256, B[b][:, 256 * j:256 * j + 256], [s.t, free[b]])
            done(s, tok)
            sg = tmp[hh]
            t0, _ = sigmoid(sg, B[b][:, :], tok, tk["f", 0], tk["f", 1])
            free[b] = V(lambda e, hh=hh, sg=sg, b=b: e.tensor_tensor(qT[:, 2 * hh:2 * hh + 2, :].rearrange("p h t -> p (h t)"),
                                                                    sg, B[b][:, :], ALU.mult), t0)
        t_q = free[b]

        tr = {}
        for d in range(2):
            for i in range(2):
                b = 4 + i
                for h in range(4):
                    tok = PE(lambda e, b=b, d=d, h=h, i=i: e.transpose(B[b][:, 128 * h:128 * h + 128],
                                                                      wctx[:, 4 * d + h, 128 * i:128 * i + 128], ident),
                             tk["b", 1], t_id, free[b])
                tr[d, i] = A(lambda e, b=b, d=d, i=i: e.activation(wtok[:, i, 512 * d:512 * d + 512], B[b][:, :], ACT.Copy), tok)
                free[b] = tr[d, i]
        for d in range(2):
            b = 6 + d
            for h in range(4):
                for i in range(2):
                    tok = PE(lambda e, b=b, d=d, h=h, i=i: e.matmul(B[b][:, 128 * h:128 * h + 128],
                                                                   wtok[:, i, 512 * d + 128 * h:512 * d + 128 * h + 128],
                                                                   vc[:, i, 128 * h:128 * h + 128], start=i == 0, stop=i == 1),
                             tr[d, 1], t_v, free[b])
            t_S = A(lambda e, b=b, d=d: e.activation(St[:, d, :], B[b][:, :], ACT.Copy), tok)
            free[b] = t_S

        def split(x, s):
            return x.rearrange("p h (n w t) -> p (h n) w t", w=2, t=s)

        t_lv = None
        pe_lv = []
        levels = [128, 64, 32, 16, 8, 4, 2, 1, 0]
        fillers = {}

        def level(li):
            nonlocal t_lv
            s = levels[li]
            wk = [pe_lv[-1]] if pe_lv else []
            if s:
                n = 1024 // (2 * s)
                F_, B_ = split(bf, s), split(bb, s)
                K_, Q_ = split(EK, s), split(EQ, s)
                rf = F_[:, :, 0, s - 1:s].broadcast_to([128, n, s])
                rb = B_[:, :, 1, 0:1].broadcast_to([128, n, s])
                V(lambda e: e.tensor_tensor(K_[:, :, 0, :], rf, F_[:, :, 0, :], ALU.subtract), tk["b", 1])
                V(lambda e: e.tensor_tensor(K_[:, :, 1, :], rb, B_[:, :, 1, :], ALU.subtract))
                V(lambda e: e.tensor_tensor(Q_[:, :, 1, :], F_[:, :, 1, :], rf, ALU.subtract))
                t = V(lambda e: e.tensor_tensor(Q_[:, :, 0, :], B_[:, :, 0, :], rb, ALU.subtract))
                ta = A(lambda e: e.activation(EK, EK, ACT.Exp), t)
                tb = A(lambda e: e.activation(EQ, EQ, ACT.Exp))
                MK_ = split(MK, s)
                V(lambda e: e.tensor_tensor(MK_[:, :, 0, :], split(kf, s)[:, :, 0, :], K_[:, :, 0, :], ALU.mult), ta, wk)
                V(lambda e: e.tensor_tensor(MK_[:, :, 1, :], split(kb, s)[:, :, 1, :], K_[:, :, 1, :], ALU.mult))
                tm = V(lambda e: e.tensor_tensor(MQ, qT, EQ, ALU.mult), tb, t_q)
                mq = MQ
            else:
                tm = V(lambda e: e.tensor_tensor(MK, kf, kb, ALU.add), wk)
                mq = qT
            if work:
                work.pop(0)()
            for j in range(2):
                i = 1 - j if s == 128 else j
                b = 4 + j
                for h in range(4):
                    tok = PE(lambda e, b=b, h=h, i=i, j=j, mq=mq: e.matmul(B[b][:, 128 * h:128 * h + 128],
                                                                          MK[:, h, 128 * j:128 * j + 128],
                                                                          mq[:, h, 128 * i:128 * i + 128], start=True, stop=True),
                             tm, free[b])
                dst = PT[:, j, :, 128 * i:128 * i + 128]
                src = B[b][:, :].rearrange("p (h i) -> p h i", h=4)
                if s >= 64:
                    free[b] = V(lambda e, dst=dst, src=src: e.tensor_copy(dst, src), tok, t_msk)
                else:
                    m = msk[:, li - 1, :].rearrange("p (o i) -> p o i", o=1).broadcast_to([128, 4, 128])
                    free[b] = V(lambda e, dst=dst, src=src, m=m: e.copy_predicated(dst, m, src), tok, t_msk)
            pe_lv.append(tok)
            t_lv = free[5]

        def gelu(dst, ps, n, pb, w, *waits):
            x1, x2 = tmp[0][:, 0:n], tmp[1][:, 0:n]
            t = A(lambda e: e.activation(x1, ps, ACT.Square), *waits, V.last())
            V(lambda e: e.tensor_scalar(x1, x1, 0.044715, 1.0, ALU.mult, ALU.add), t)
            V(lambda e: e.tensor_tensor(x2, x1, ps, ALU.mult))
            t = V(lambda e: e.tensor_scalar(x2, x2, -43.0 / GELU_C, None, ALU.max))
            A(lambda e: e.activation(x2, x2, ACT.Exp, scale=-GELU_C), t)
            A(lambda e: e.activation(x2, x2, ACT.Ln, bias=ones[:, 0:1]))
            t = A(lambda e: e.activation(x2, x2, ACT.Exp, scale=-1.0))
            return V(lambda e: e.tensor_tensor(dst, x2, ps, ALU.mult), t)

        def p_sv(hh):
            s = wslot(win, SO + 256 * hh)
            for i in range(2):
                b = nextbank()
                for k in range(8):
                    tok = PE(lambda e, k=k, b=b, s=s, i=i: e.matmul(B[b][:, 0:256], HT[:, k, 256 + 128 * i:384 + 128 * i], s.v[:, k, :],
                                                                    start=k == 0, stop=k == 7), s.t, free[b])
                free[b] = gelu(svt[:, i, 256 * hh:256 * hh + 256], B[b][:, 0:256], 256, None, None, tok)
            done(s, tok)

        def p_two(off, hh, fn):
            s = wslot(win, off + 256 * hh)
            b = nextbank()
            for j in range(2):
                tok = projT(s.v, s, slice(128 * j, 128 * j + 128), Hx, 256, B[b][:, 256 * j:256 * j + 256], [s.t, free[b]])
            done(s, tok)
            free[b] = fn(hh, B[b][:, :], tok)

        def e_u(hh, ps, tok):
            return gelu(uT[:, 2 * hh:2 * hh + 2, :].rearrange("p h t -> p (h t)"), ps, 512, None, None, tok)

        def e_g(hh, ps, tok):
            dst = gT[:, 2 * hh:2 * hh + 2, :].rearrange("p h t -> p (h t)")
            t, _ = sigmoid(dst, ps, tok)
            return V(lambda e: e.tensor_tensor(dst, dst, ps, ALU.mult), t)

        def e_s(buf):
            def f(hh, ps, tok):
                dst = buf[:, 2 * hh:2 * hh + 2, :].rearrange("p h t -> p (h t)")
                t, w = sigmoid(dst, ps, tok)
                return w
            return f

        work = [lambda: p_sv(0), lambda: p_sv(1), lambda: p_two(UO, 0, e_u), lambda: p_two(UO, 1, e_u),
                lambda: p_two(GO, 0, e_g), lambda: p_two(GO, 1, e_g)]
        work += [lambda i=i: p_two(AO, i, e_s(SA)) for i in range(4)] + [lambda i=i: p_two(CO, i, e_s(SB)) for i in range(4)]
        for li in range(len(levels)):
            level(li)

        tq = []
        for d, bx, ex in ((0, bf, EK), (1, bb, EQ)):
            t = A(lambda e, bx=bx, ex=ex: e.activation(ex, bx, ACT.Exp), V.last())
            tq.append(V(lambda e, ex=ex: e.tensor_tensor(ex, ex, qT, ALU.mult), t))
        t_o = []
        for h in range(4):
            b = 6 + h // 2
            po = B[b][:, 256 * (h % 2):256 * (h % 2) + 256]
            hs = slice(128 * h, 128 * h + 128)
            tok = PE(lambda e, po=po, h=h, hs=hs: e.matmul(po, St[:, 0, hs], EK[:, h, :], start=True, stop=False), t_S, tq, free[b])
            PE(lambda e, po=po, h=h, hs=hs: e.matmul(po, St[:, 1, hs], EQ[:, h, :], start=False, stop=False))
            PE(lambda e, po=po, h=h, hs=hs: e.matmul(po, vx[:, 0, hs], PT[:, 0, h, :], start=False, stop=False), t_lv)
            tok = PE(lambda e, po=po, h=h, hs=hs: e.matmul(po, vx[:, 1, hs], PT[:, 1, h, :], start=False, stop=True))
            if h % 2:
                ov = oT[:, h - 1:h + 1, :].rearrange("p h t -> p (h t)")
                t = V(lambda e, ov=ov, b=b: e.tensor_copy(ov, B[b][:, :]), tok)
                free[b] = t
                sq = tmp[2 + h // 2]
                ta = A(lambda e, ov=ov, sq=sq: e.activation(sq, ov, ACT.Square), t)
                t_o.append((h, ta, sq, ov))
        if work:
            work.pop(0)()
        for h, ta, sq, ov in t_o:
            b = 4 + h // 2
            tok = PE(lambda e, b=b, sq=sq: e.matmul(B[b][:, :], ones, sq, start=True, stop=True), ta, free[b])
            t = rstd(sq, B[b][:, :], 128, tok)
            free[b] = t
            V(lambda e, ov=ov, sq=sq: e.tensor_tensor(ov, ov, sq, ALU.mult), t)
            for j in (h - 1, h):
                t_oT = V(lambda e, j=j: e.scalar_tensor_tensor(oT[:, j, :], oT[:, j, :], vc_("hgn", j), gT[:, j, :], ALU.mult, ALU.mult))
        while len(work) > 2:
            work.pop(0)()

        for i in range(2):
            sv = svt[:, i, :]
            V(lambda e, sv=sv: e.tensor_tensor(tmp[2], sv, sv, ALU.mult))
            ss = ctmp[:, 4 * i:4 * i + 4]
            t = V(lambda e, ss=ss: e.tensor_reduce(ss, tmp[2].rearrange("p (g c) -> p g c", g=4), AX, ALU.add))
            t = rstd(ss, ss, 128, t)
            sg = sv.rearrange("p (g c) -> p g c", g=4)
            t_sv = V(lambda e, sg=sg, ss=ss: e.tensor_tensor(sg, sg, ss.rearrange("p (g o) -> p g o", o=1).broadcast_to([128, 4, 128]),
                                                             ALU.mult), t)
        for g in range(4):
            for i in range(2):
                o0 = 256 * (g % 2) + 128 * i
                tok = PE(lambda e, b=4 + g // 2, g=g, i=i, o0=o0: e.matmul(
                    B[b][:, o0:o0 + 128], svt[:, i, 128 * g:128 * g + 128], wst[:, g, :], start=True, stop=True),
                    t_sv, t_wst, free[4 + g // 2])
            if g % 2 == 0:
                continue
            for gg in (g - 1, g):
                pv = B[4 + g // 2][:, 256 * (gg % 2):256 * (gg % 2) + 256].rearrange("p (i t) -> p i t", i=2)
                bs = bsb[:, gg:gg + 1, :].broadcast_to([128, 2, 128])
                m = tmp[3][:, 0:256].rearrange("p (i t) -> p i t", i=2)
                t = V(lambda e, pv=pv, bs=bs, m=m, gg=gg: e.scalar_tensor_tensor(m, pv, vc_("sgn", gg), bs, ALU.mult, ALU.add),
                      tok, t_bsb)
                t_uT = V(lambda e, gg=gg: e.tensor_tensor(uT[:, gg, :], uT[:, gg, :], tmp[3][:, 0:256], ALU.mult))
            free[4 + g // 2] = t
        while work:
            work.pop(0)()
        t_hdone = PE.last()
        t_sab = [V.last(), A.last()]

        t_a1 = ada(1)
        t_a2 = ada(2)

        wa = a["w_branch_a"].rearrange("(k p) n -> p k n", p=128)
        wb = a["w_branch_b"].rearrange("(k p) n -> p k n", p=128)
        for c in range(2):
            s1 = stream(wa[:, :, 512 * c:512 * c + 512], [4, 512])
            s2 = stream(wb[:, :, 512 * c:512 * c + 512], [4, 512])
            for j in range(4):
                db = 4 * c + j
                b = nextbank()
                tok = projT(s1.v, s1, slice(128 * j, 128 * j + 128), lambda k: oT[:, k, :], 256, B[b][:, 0:256],
                            [s1.t, free[b], t_oT], kn=4)
                if j == 3:
                    done(s1, tok)
                tok = projT(s2.v, s2, slice(128 * j, 128 * j + 128), lambda k: uT[:, k, :], 256, B[b][:, 256:512],
                            [s2.t, t_uT], kn=4)
                if j == 3:
                    done(s2, tok)
                V(lambda e, b=b, db=db: e.tensor_tensor(tmp[4][:, 0:256], SA[:, db, :], B[b][:, 0:256], ALU.mult), tok, t_sab)
                free[b] = V(lambda e, b=b, db=db: e.tensor_tensor(tmp[4][:, 256:512], SB[:, db, :], B[b][:, 256:512], ALU.mult))
                t_mg = V(lambda e, db=db: e.tensor_tensor(MG[:, db, :], tmp[4][:, 0:256], tmp[4][:, 256:512], ALU.add), t_hdone)
        wo = a["w_out"].rearrange("(k p) n -> p k n", p=128)

        def wout(src, X, lhs_in, wait, gate):
            tt = None
            for c in range(4):
                s = wslot(src, 256 * c)
                b = nextbank()
                for j in range(2):
                    tok = projT(s.v, s, slice(128 * j, 128 * j + 128), lhs_in, 256, B[b][:, 256 * j:256 * j + 256], [s.t, free[b], wait])
                done(s, tok)
                for j in range(2):
                    db = 2 * c + j
                    ps = B[b][:, 256 * j:256 * j + 256]
                    if gate is not None:
                        tt = V(lambda e, db=db, ps=ps: e.scalar_tensor_tensor(X[:, db, :], ps, gate(db), X[:, db, :], ALU.mult, ALU.add), tok)
                    else:
                        tt = V(lambda e, db=db, ps=ps: e.tensor_tensor(X[:, db, :], ps, X[:, db, :], ALU.add), tok)
                free[b] = tt
            return tt

        t_x1 = wout(wo, XX, lambda k: MG[:, k, :], t_mg, lambda db: mod[:, 16 + db, 0:1])
        late_tok = [PE.last(), V.last(), A.last()]

        z2 = [late]
        H2 = new(2048, z2).rearrange("p (k t) -> p k t", k=8)
        H2k = new(2048, z2).rearrange("p (i n) -> p i n", i=2)
        XS = new(4096, z2).rearrange("p (k n) -> p k n", k=8)
        Pm = new(1024, z2).rearrange("p (i e s) -> p i e s", i=2, e=16)
        PR = [new(256, z2).rearrange("p (i r s) -> p i r s", i=2, r=4) for _ in range(2)]
        MOE = new(2048, z2).rearrange("p (k t) -> p k t", k=8)
        Gt = [new(256, z2) for _ in range(2)]
        hid = [new(512, z2) for _ in range(2)]
        sgm = new(512, z2)
        hidT = [new(512, z2) for _ in range(2)]
        YE = [H2[:, 4 * i:4 * i + 4, :].rearrange("p k t -> p (k t)") for i in range(2)]
        af = new(256, z2)
        wk_ = new(256, z2)
        lgt = new(256, z2)
        m8 = new(32, z2)
        affk = new(32, z2).rearrange("p (i n) -> p i n", i=2)
        posk = new(32, z2).rearrange("p (i n) -> p i n", i=2)
        sm = new(64, z2)
        sq2 = MOE.rearrange("p k t -> p (k t)")
        rs2 = new(256, z2)

        def norm(X, dst, n, tx, scale, shift, SQb, rsb, bank, *w):
            sqv = SQb.rearrange("p (k t) -> p k t", k=8)
            t = A(lambda e: e.activation(sqv, X, ACT.Square), tx, *w)
            V(lambda e: e.tensor_tensor(sqv[:, 0:4, :], sqv[:, 0:4, :], sqv[:, 4:8, :], ALU.add), t)
            V(lambda e: e.tensor_tensor(sqv[:, 0:2, :], sqv[:, 0:2, :], sqv[:, 2:4, :], ALU.add))
            t = V(lambda e: e.tensor_tensor(sqv[:, 0, :], sqv[:, 0, :], sqv[:, 1, :], ALU.add))
            tok = PE(lambda e: e.matmul(B[bank][:, 0:256], ones, sqv[:, 0, :], start=True, stop=True), t, free[bank])
            t = rstd(rsb, B[bank][:, 0:256], D, tok)
            free[bank] = t
            out_ = []
            for k in range(8):
                tv = V(lambda e, k=k: e.scalar_tensor_tensor(dst[:, k, :], X[:, k, :], scale(k), rsb, ALU.mult, ALU.mult), t)
                if shift is not None:
                    tv = A(lambda e, k=k: e.activation(dst[:, k, :], dst[:, k, :], ACT.Identity, bias=shift(k)), tv)
                out_.append(tv)
            return out_

        V(lambda e: e.scalar_tensor_tensor(swf, mod[:, 32:40, 0], 1.0, vc_("nffn", 0, 8), ALU.add, ALU.mult))
        t_h2 = norm(XX, H2, D, t_x1, lambda k: swf[:, k:k + 1], lambda k: mod[:, 24 + k, 0:1], sq2, rs2, 4, late_tok)

        for k in range(8):
            tok = PE(lambda e, k=k: e.matmul(B[5][0:16, 0:256], wr[:, k, :], H2[:, k, :], start=k == 0, stop=k == 7),
                     t_h2[k], t_wr, free[5])
        t = V(lambda e: e.tensor_copy(lgt[0:16, :], B[5][0:16, 0:256]), tok)
        free[5] = t
        for i in range(2):
            tok = PE(lambda e, i=i: e.transpose(B[6][:, 16 * i:16 * i + 16], lgt[0:16, 128 * i:128 * i + 128], ident[0:16, 0:16]), t, free[6])
        lp = B[6][:, 0:32].rearrange("p (i n) -> p i n", i=2)
        bc = lambda x: x.rearrange("p (i o) -> p i o", o=1).broadcast_to([128, 2, 16])
        V(lambda e: e.tensor_reduce(sm[:, 0:2], lp, AX, ALU.max), tok)
        t = V(lambda e: e.tensor_tensor(affk, lp, bc(sm[:, 0:2]), ALU.subtract))
        free[6] = t
        t = A(lambda e: e.activation(affk, affk, ACT.Exp), t)
        V(lambda e: e.tensor_reduce(sm[:, 2:4], affk, AX, ALU.add), t)
        V(lambda e: e.reciprocal(sm[:, 4:6], sm[:, 2:4]))
        t_aff = V(lambda e: e.tensor_tensor(affk, affk, bc(sm[:, 4:6]), ALU.mult))
        for i in range(2):
            tok = PE(lambda e, i=i: e.transpose(B[6][0:16, 128 * i:128 * i + 128], affk[:, i, :], ident), t_aff, free[6])
        for i in range(2):
            for c in range(2):
                b = (0, 1, 2, 3)[2 * i + c]
                for j in range(4):
                    k = 4 * c + j
                    tk2 = PE(lambda e, b=b, i=i, j=j, k=k: e.transpose(B[b][:, 128 * j:128 * j + 128], H2[:, k, 128 * i:128 * i + 128], ident),
                             t_h2[-1], free[b])
                t_h2k = A(lambda e, b=b, i=i, c=c: e.activation(H2k[:, i, 512 * c:512 * c + 512], B[b][:, :], ACT.Copy), tk2)
                free[b] = t_h2k
        w16 = wk_[0:16, :]
        t = V(lambda e: e.tensor_copy(w16, B[6][0:16, 0:256]), tok)
        free[6] = t
        for r in range(4):
            V(lambda e, r=r: e.max(m8[0:16, 8 * r:8 * r + 8], w16))
            V(lambda e, r=r: e.match_replace(w16, m8[0:16, 8 * r:8 * r + 8], w16, -1.0))
        V(lambda e: e.tensor_scalar(w16, w16, 0.0, None, ALU.is_lt))
        V(lambda e: e.tensor_tensor_scan(af[0:16, :], ones[0:16, 0:1].broadcast_to([16, 256]), w16, 0.0, ALU.mult, ALU.add))
        t = V(lambda e: e.tensor_tensor(af[0:16, :], af[0:16, :], w16, ALU.mult))
        for i in range(2):
            tok = PE(lambda e, i=i: e.transpose(B[6][:, 16 * i:16 * i + 16], af[0:16, 128 * i:128 * i + 128], ident[0:16, 0:16]), t, free[6])
        t = V(lambda e: e.tensor_copy(posk, lp), tok)
        free[6] = t
        io = iot.rearrange("p (o s) -> p o s", o=1).broadcast_to([128, 16, 32])
        for i in range(2):
            t_P = V(lambda e, i=i: e.tensor_tensor(Pm[:, i, :, :], io, posk[:, i, :].rearrange("p (n o) -> p n o", o=1)
                                                   .broadcast_to([128, 16, 32]), ALU.is_equal), t_iot)
        t_xs = {}

        def gather(half):
            for k in range(8):
                b = 6 + k % 2
                for i in range(2):
                    tok = PE(lambda e, b=b, i=i, k=k: e.matmul(B[b][:, 0:256], H2k[:, i, 128 * k:128 * k + 128],
                                                               Pm[:, i, 8 * half:8 * half + 8, :], start=i == 0, stop=i == 1),
                             t_P, t_h2k, free[b])
                f = lambda e, b=b, k=k: e.activation(XS[:, k, 256 * half:256 * half + 256], B[b][:, 0:256], ACT.Copy)
                free[b] = A(f, tok)
                t_xs[half] = free[b]

        gather(0)

        for i in range(MORE_SLOTS):
            s = Slot()
            s.free = late_tok
            last_done[BASE_SLOTS + i] = s
        ring[:] = [x for i in range(BASE_SLOTS) for x in (i, BASE_SLOTS + i)]
        nx = at[0] % BASE_SLOTS
        ring[:] = ring[2 * nx:] + ring[:2 * nx]
        at[0] = 0
        wg, wu = a["wg"], a["wu"]
        wd = a["wd"].rearrange("e (j c p) n -> e c p j n", j=4, c=4)
        GB, UB, TB, D0, D1, S0, S1 = 0, 1, 2, 3, 4, 5, 6
        y_tok, sc_free, moe_tok = {}, [None, None], None
        g_tok, pe_sc, hid_pe, h2_pe, g_pe = {}, {}, {}, {}, {}
        NEX = NE

        def prep_g(e_):
            pr = PR[e_ % 2]
            tp = G(lambda e: e.tensor_tensor(pr, Pm[:, :, e_:e_ + 1, :].broadcast_to([128, 2, 4, 32]),
                                             affk[:, :, e_:e_ + 1].rearrange("p i (n o) -> p i n o", o=1).broadcast_to([128, 2, 4, 32]),
                                             ALU.mult), t_P, g_pe.get(e_ - 2))
            for i in range(2):
                tok = PE(lambda e, i=i: e.transpose(B[7][:, 128 * i:128 * i + 128], pr[:, i, :, :].rearrange("p r s -> p (r s)"), ident),
                         tp, free[7])
            g_pe[e_] = tok
            g_tok[e_] = A(lambda e: e.activation(Gt[e_ % 2], B[7][:, 0:256], ACT.Copy), tok, pe_sc.get(e_ - 2))
            free[7] = g_tok[e_]

        def scatter(e_):
            nonlocal moe_tok
            for q in range(4):
                b = (S0, S1)[q % 2]
                for j in range(2):
                    db = 2 * q + j
                    tok = PE(lambda e, b=b, j=j, db=db: e.matmul(B[b][:, 256 * j:256 * j + 256], YE[e_ % 2][:, 128 * db:128 * db + 128],
                                                                 Gt[e_ % 2], start=True, stop=True),
                             y_tok[e_], g_tok[e_], free[b])
                mv = MOE[:, 2 * q:2 * q + 2, :].rearrange("p k t -> p (k t)")
                if e_ == 0:
                    free[b] = V(lambda e, b=b, mv=mv: e.tensor_copy(mv, B[b][:, :]), tok)
                else:
                    free[b] = V(lambda e, b=b, mv=mv: e.tensor_tensor(mv, mv, B[b][:, :], ALU.add), tok)
            pe_sc[e_] = tok
            moe_tok = free[b]

        def up(src, e_, bank, hook=None):
            for k in range(8):
                s = stream(src[e_, k * 128:(k + 1) * 128, :], [2048])
                for j in range(4):
                    tok = PE(lambda e, k=k, j=j, s=s: e.matmul(B[bank][32 * j:32 * j + 32, :], XS[:, k, 32 * e_:32 * e_ + 32],
                                                               s.v[:, 512 * j:512 * j + 512], start=k == 0, stop=k == 7),
                             s.t, t_xs[e_ // 8], free[bank])
                done(s, tok)
                if hook and k == 3:
                    hook()
            return tok

        for e_ in range(NEX):
            tg = up(wg, e_, GB, (lambda: scatter(e_ - 1)) if e_ else None)
            if e_ == 0:
                gather(1)
            prep_g(e_)
            t, _ = sigmoid(sgm, B[GB][:, :], tg)
            hd, hT_ = hid[e_ % 2], hidT[e_ % 2]
            free[GB] = V(lambda e: e.tensor_tensor(sgm, sgm, B[GB][:, :], ALU.mult), t)
            tu = up(wu, e_, UB)
            t = V(lambda e, hd=hd: e.tensor_tensor(hd, sgm, B[UB][:, :], ALU.mult), tu, hid_pe.get(e_ - 2))
            free[UB] = t
            for c in range(4):
                tok = PE(lambda e, c=c, hd=hd: e.transpose(B[TB][:, 128 * c:128 * c + 128], hd[:, 128 * c:128 * c + 128], ident), t, free[TB])
            hid_pe[e_] = tok
            th = A(lambda e, hT_=hT_: e.activation(hT_, B[TB][:, :], ACT.Copy), tok, h2_pe.get(e_ - 2))
            free[TB] = th
            for c in range(4):
                ss = [stream(wd[e_, c, :, 2 * jj:2 * jj + 2, :], [2, 1024]) for jj in range(2)]
                for db in range(2):
                    for j in range(4):
                        tok = PE(lambda e, c=c, j=j, db=db, s=ss[j // 2], hT_=hT_: e.matmul(
                            B[(D0, D1)[db]][32 * j:32 * j + 32, :], hT_[:, 128 * c + 32 * j:128 * c + 32 * j + 32],
                            s.v[:, j % 2, 512 * db:512 * db + 512], start=c == 0, stop=c == 3),
                            ss[j // 2].t, th, free[D0], free[D1])
                for s in ss:
                    done(s, tok)
            h2_pe[e_] = tok
            ye = YE[e_ % 2]
            free[D0] = A(lambda e, ye=ye: e.activation(ye[:, 0:512], B[D0][:, :], ACT.Copy), tok, pe_sc.get(e_ - 2))
            free[D1] = V(lambda e, ye=ye: e.tensor_copy(ye[:, 512:1024], B[D1][:, :]), tok, pe_sc.get(e_ - 2))
            y_tok[e_] = [free[D0], free[D1]]
        if NEX:
            scatter(NEX - 1)
            for k in range(8):
                t_x2 = V(lambda e, k=k: e.scalar_tensor_tensor(XX[:, k, :], MOE[:, k, :], mod[:, 40 + k, 0:1], XX[:, k, :], ALU.mult, ALU.add))

        z3 = [zone]
        HN = new(2048, z3).rearrange("p (k t) -> p k t", k=8)
        ZA = new(2048, z3).rearrange("p (k t) -> p k t", k=8)
        C2 = new(2048, z3).rearrange("p (k t) -> p k t", k=8)
        UU = new(8 * 258, z3).rearrange("p (k t) -> p k t", k=8)
        GA = new(2048, z3).rearrange("p (k t) -> p k t", k=8)
        GC = new(2048, z3).rearrange("p (k t) -> p k t", k=8)
        vk = new(2048, z3).rearrange("p (i n) -> p i n", i=2)
        o2 = new(2048, z3).rearrange("p (k t) -> p k t", k=8)
        PT2 = new(2048, z3)
        q2 = new(1024, z3).rearrange("p (h t) -> p h t", h=4)
        k2 = new(1024, z3).rearrange("p (h t) -> p h t", h=4)
        b2 = new(1024, z3).rearrange("p (h t) -> p h t", h=4)
        E2 = [new(1024, z3).rearrange("p (h t) -> p h t", h=4) for _ in range(2)]
        M2 = [new(1024, z3).rearrange("p (h t) -> p h t", h=4) for _ in range(2)]
        tp2 = [new(512, z3) for _ in range(6)]
        gkl = new(256, z3)
        rs3 = new(256, z3)
        SQ3 = new(2048, z3)
        MG2 = PT2.rearrange("p (k t) -> p k t", k=8)
        PTv = PT2.rearrange("p (j h i) -> p j h i", j=2, h=4)
        ring[:] = list(range(BASE_SLOTS))
        at[0] = 0
        quiet = [PE.last(), V.last(), A.last(), G.last()]
        t = norm(XX, XX, D, t_x2, lambda k: vc_("fnw", k), None, SQ3, rs3, 4, quiet)
        t_hn = norm(XX, HN, D, t, lambda k: vc_("nm2", k), None, SQ3, rs3, 4)
        V(lambda e: e.memset(UU[:, :, 0:2], 0.0))
        z_pt = V(lambda e: e.memset(PT2, 0.0))
        w2 = a["w_in2"].rearrange("(k p) n -> p k n", p=128)
        Hn = lambda k: HN[:, k, :]

        s = stream(w2[:, :, 3072:3088], [8, 16])
        for k in range(8):
            tok = PE(lambda e, k=k, s=s: e.matmul(B[4][0:16, 0:256], s.v[:, k, :], HN[:, k, :], start=k == 0, stop=k == 7),
                     s.t, t_hn[k], free[4])
        done(s, tok)
        t = free[4] = V(lambda e: e.tensor_copy(gkl[0:16, :], B[4][0:16, 0:256]), tok)
        s = stream(a["w_gk2"], [512], parts=16)
        for h in range(4):
            tok = PE(lambda e, h=h, s=s: e.matmul(B[6 + h // 2][:, 256 * (h % 2):256 * (h % 2) + 256], s.v[:, 128 * h:128 * h + 128],
                                                  gkl[0:16, :], start=True, stop=True), s.t, t, free[6], free[7])
        done(s, tok)
        onr = ones[:, 0:1].broadcast_to([128, 256])
        for u in range(2):
            zz, aa = tp2[2 * u], tp2[2 * u + 1]
            for j in range(2):
                t = V(lambda e, j=j, u=u, zz=zz: e.tensor_scalar(zz[:, 256 * j:256 * j + 256], B[6 + u][:, 256 * j:256 * j + 256],
                                                                vc_("bgk", 2 * u + j), None, ALU.add), tok)
            free[6 + u] = t
            t = V(lambda e, zz=zz, aa=aa: e.scalar_tensor_tensor(aa, zz, -1.0, zz, ALU.mult, ALU.max))
            A(lambda e, aa=aa: e.activation(aa, aa, ACT.Exp, scale=-1.0), t)
            t = A(lambda e, aa=aa: e.activation(aa, aa, ACT.Ln, bias=ones[:, 0:1]))
            V(lambda e, zz=zz, aa=aa: e.scalar_tensor_tensor(aa, zz, 0.0, aa, ALU.min, ALU.subtract), t)
            for j in range(2):
                t_b2 = V(lambda e, aa=aa, u=u, j=j: e.tensor_tensor_scan(b2[:, 2 * u + j, :], onr, aa[:, 256 * j:256 * j + 256],
                                                                        0.0, ALU.mult, ALU.add))

        def p2(off, hh, fn, kn=8):
            s = wslot(w2, off + 256 * hh)
            b = nextbank()
            for j in range(2):
                tok = projT(s.v, s, slice(128 * j, 128 * j + 128), Hn, 256, B[b][:, 256 * j:256 * j + 256], [s.t, t_hn, free[b]])
            done(s, tok)
            free[b] = fn(hh, B[b][:, :], tok)
            return free[b]

        pair = lambda x, hh: x[:, 2 * hh:2 * hh + 2, :].rearrange("p h t -> p (h t)")
        for hh in range(2):
            t_q2 = p2(0, hh, lambda hh, ps, tok: A(lambda e: e.activation(pair(q2, hh), ps, ACT.Copy, scale=128 ** -0.5), tok))
        for hh in range(2):
            t_k2 = p2(512, hh, lambda hh, ps, tok: A(lambda e: e.activation(pair(k2, hh), ps, ACT.Copy), tok))
        for hh in range(4):
            s = wslot(w2, 1024 + 256 * hh)
            for i in range(2):
                b = nextbank()
                for k in range(8):
                    tok = PE(lambda e, k=k, b=b, s=s, i=i: e.matmul(B[b][:, 0:256], HN[:, k, 128 * i:128 * i + 128], s.v[:, k, :],
                                                                    start=k == 0, stop=k == 7), s.t, free[b])
                t_v2 = free[b] = A(lambda e, b=b, i=i, hh=hh: e.activation(vk[:, i, 256 * hh:256 * hh + 256], B[b][:, 0:256], ACT.Copy), tok)
            done(s, tok)

        K_, Q_ = E2
        MK_, MQ_ = M2
        I16 = 1.0 / 16.0
        last_mm = None
        for s_ in (128, 64):
            n = 1024 // (2 * s_)
            bv = split(b2, s_)
            Kv, Qv = split(K_, s_), split(Q_, s_)
            r = bv[:, :, 0, s_ - 1:s_].broadcast_to([128, n, s_])
            V(lambda e, r=r, Kv=Kv, bv=bv: e.tensor_tensor(Kv[:, :, 0, :], r, bv[:, :, 0, :], ALU.subtract))
            t = V(lambda e, r=r, Qv=Qv, bv=bv: e.tensor_tensor(Qv[:, :, 1, :], bv[:, :, 1, :], r, ALU.subtract))
            A(lambda e, Kv=Kv: e.activation(Kv[:, :, 0, :], Kv[:, :, 0, :], ACT.Exp, scale=I16), t)
            t = A(lambda e, Qv=Qv: e.activation(Qv[:, :, 1, :], Qv[:, :, 1, :], ACT.Exp, scale=I16))
            V(lambda e, Kv=Kv, s_=s_: e.tensor_tensor(split(MK_, s_)[:, :, 0, :], split(k2, s_)[:, :, 0, :], Kv[:, :, 0, :], ALU.mult),
              t, t_k2, t_q2, last_mm)
            t = V(lambda e, Qv=Qv, s_=s_: e.tensor_tensor(split(MQ_, s_)[:, :, 1, :], split(q2, s_)[:, :, 1, :], Qv[:, :, 1, :], ALU.mult))
            for j in range(1 if s_ == 128 else 2):
                for h in range(4):
                    if s_ == 128:
                        o_, lh, rh = B[4][:, 128 * h:128 * h + 128], MK_[:, h, 0:128], MQ_[:, h, 128:256]
                    else:
                        c0 = 256 * j + 64 * h
                        o_, lh, rh = B[5][0:64, c0:c0 + 64], MK_[:, h, 128 * j:128 * j + 64], MQ_[:, h, 128 * j + 64:128 * j + 128]
                    tok = PE(lambda e, o_=o_, lh=lh, rh=rh: e.matmul(o_, lh, rh, start=True, stop=True), t, free[4], free[5])
            last_mm = tok
            if s_ == 128:
                free[4] = V(lambda e: e.tensor_copy(PTv[:, 0, :, 128:256], B[4].rearrange("p (h i) -> p h i", h=4)), tok, z_pt)
            else:
                for j in range(2):
                    free[5] = V(lambda e, j=j: e.tensor_copy(PTv[0:64, j, :, 128 * j + 64:128 * j + 128],
                                                             B[5][0:64, 256 * j:256 * j + 256].rearrange("p (h i) -> p h i", h=4)), tok)
        bc4 = b2.rearrange("p h (n t) -> p h n t", n=4)
        K4 = K_.rearrange("p h (n t) -> p h n t", n=4)
        V(lambda e: e.tensor_copy(K4[:, :, 0, :], bc4[:, :, 0, :]))
        t = V(lambda e: e.tensor_tensor(K4[:, :, 1:4, :], bc4[:, :, 1:4, :], bc4[:, :, 0:3, 63:64].broadcast_to([128, 4, 3, 64]), ALU.subtract))
        A(lambda e: e.activation(Q_, K_, ACT.Exp, scale=I16), t)
        t = A(lambda e: e.activation(K_, K_, ACT.Exp, scale=-I16))
        V(lambda e: e.tensor_tensor(MK_, k2, K_, ALU.mult), t, last_mm)
        t = V(lambda e: e.tensor_tensor(MQ_, q2, Q_, ALU.mult))
        for j in range(2):
            for h in range(4):
                tok = PE(lambda e, j=j, h=h: e.matmul(B[4 + j][:, 128 * h:128 * h + 128], MK_[:, h, 128 * j:128 * j + 128],
                                                      MQ_[:, h, 128 * j:128 * j + 128], start=True, stop=True), t, free[4], free[5])
            lm = msk[:, 8, :].rearrange("p (o i) -> p o i", o=1).broadcast_to([128, 4, 128])
            t_pt2 = V(lambda e, j=j, lm=lm: e.copy_predicated(PTv[:, j, :, 128 * j:128 * j + 128], lm,
                                                              B[4 + j].rearrange("p (h i) -> p h i", h=4)), tok)
            free[4 + j] = t_pt2

        CC, XO, CB, ZC, ZO, GAO, GCO = 4112, 5136, 3088, 6160, 2048, 7184, 8208
        for hh in range(4):
            t_cc = p2(CC, hh, lambda hh, ps, tok: A(lambda e: e.activation(pair(C2, hh), ps, ACT.Copy), tok))

        def e_x(hh, ps, tok):
            u = UU[:, 2 * hh:2 * hh + 2, 2:258]
            r = V(lambda e: e.tensor_tensor(u, C2[:, 2 * hh:2 * hh + 2, :], ps.rearrange("p (h t) -> p h t", h=2), ALU.mult), tok, t_cc)
            for k in (2 * hh, 2 * hh + 1):
                V(lambda e, k=k: e.tensor_scalar(C2[:, k, :], UU[:, k, 2:258], vc_("cw", 16 + k), None, ALU.mult))
                for w in (1, 0):
                    V(lambda e, k=k, w=w: e.scalar_tensor_tensor(C2[:, k, :], UU[:, k, w:w + 256], vc_("cw", 8 * w + k), C2[:, k, :],
                                                                 ALU.mult, ALU.add))
            return r

        for hh in range(4):
            p2(XO, hh, e_x)
        for hh in range(4):
            p2(CB, hh, lambda hh, ps, tok: V(lambda e: e.tensor_tensor(pair(C2, hh), pair(C2, hh), ps, ALU.mult), tok))

        def silu_ps(dst, ps, tok, into=None):
            t, _ = sigmoid(dst, ps, tok, V.last())
            r = V(lambda e: e.tensor_tensor(dst, dst, ps, ALU.mult), t)
            if into is not None:
                V(lambda e: e.tensor_tensor(into, into, dst, ALU.mult))
            return r

        for hh in range(4):
            p2(ZC, hh, lambda hh, ps, tok: silu_ps(tp2[hh % 2], ps, tok, pair(C2, hh)))
        t_c2 = V.last()

        for h in range(4):
            b = 4 + h % 2
            for w in range(2):
                ps = B[b][:, 256 * w:256 * w + 256]
                vs = slice(256 * h + 128 * w, 256 * h + 128 * w + 128)
                PE(lambda e, ps=ps, h=h, vs=vs: e.matmul(ps, vk[:, 0, vs], PTv[:, 0, h, :], start=True, stop=False), t_pt2, t_v2, free[b])
                tok = PE(lambda e, ps=ps, h=h, vs=vs: e.matmul(ps[:, 128:256], vk[:, 1, vs], PTv[:, 1, h, 128:256], start=False, stop=True))
            ov = pair(o2, h)
            t = free[b] = V(lambda e, ov=ov, b=b: e.tensor_copy(ov, B[b]), tok)
            sq = tp2[2 + h]
            t = A(lambda e, ov=ov, sq=sq: e.activation(sq, ov, ACT.Square), t)
            for w in range(2):
                tok = PE(lambda e, h=h, w=w, sq=sq: e.matmul(B[6 + h // 2][:, 256 * (h % 2):256 * (h % 2) + 256], ones,
                                                            sq[:, 256 * w:256 * w + 256], start=w == 0, stop=w == 1), t, free[6 + h // 2])
            if h % 2:
                u = h // 2
                r = tp2[u]
                t = free[6 + u] = rstd(r, B[6 + u], 256, tok, V.last())
                for hx in (h - 1, h):
                    rv = r[:, 256 * (hx % 2):256 * (hx % 2) + 256]
                    for w in range(2):
                        t_o2 = V(lambda e, hx=hx, w=w, rv=rv: e.scalar_tensor_tensor(o2[:, 2 * hx + w, :], o2[:, 2 * hx + w, :], vc_("gng", w), rv,
                                                                                    ALU.mult, ALU.mult), t)
        for hh in range(4):
            p2(ZO, hh, lambda hh, ps, tok: silu_ps(pair(ZA, hh), ps, tok, pair(o2, hh)))
        t_o2 = V.last()

        def e_gate(buf, off):
            def f(hh, ps, tok):
                for j in range(2):
                    k = 2 * hh + j
                    w = V(lambda e, j=j, k=k: e.tensor_scalar(buf[:, k, :], ps[:, 256 * j:256 * j + 256], vc_("bm2", off + k), -43.0,
                                                              ALU.add, ALU.max), tok)
                pv = pair(buf, hh)
                A(lambda e: e.activation(pv, pv, ACT.Exp, scale=-1.0), w)
                A(lambda e: e.activation(pv, pv, ACT.Ln, bias=ones[:, 0:1]))
                A(lambda e: e.activation(pv, pv, ACT.Exp, scale=-1.0))
                return w
            return f

        for hh in range(4):
            p2(GAO, hh, e_gate(GA, 0))
        for hh in range(4):
            p2(GCO, hh, e_gate(GC, 8))
        t_gg = A.last()
        wa2 = a["wa2"].rearrange("(k p) n -> p k n", p=128)
        wc2 = a["wc2"].rearrange("(k p) n -> p k n", p=128)
        t_pt_read = PE.last()
        for c in range(4):
            sa_, sc_ = wslot(wa2, 256 * c), wslot(wc2, 256 * c)
            for j in range(2):
                db = 2 * c + j
                b = nextbank()
                tok = projT(sa_.v, sa_, slice(128 * j, 128 * j + 128), lambda k: o2[:, k, :], 256, B[b][:, 0:256], [sa_.t, free[b], t_o2])
                if j:
                    done(sa_, tok)
                tok = projT(sc_.v, sc_, slice(128 * j, 128 * j + 128), lambda k: C2[:, k, :], 256, B[b][:, 256:512], [sc_.t, t_c2])
                if j:
                    done(sc_, tok)
                V(lambda e, b=b, db=db: e.tensor_tensor(tp2[4][:, 0:256], GA[:, db, :], B[b][:, 0:256], ALU.mult), tok, t_gg)
                free[b] = V(lambda e, b=b, db=db: e.tensor_tensor(tp2[4][:, 256:512], GC[:, db, :], B[b][:, 256:512], ALU.mult))
                t_mg = V(lambda e, db=db: e.tensor_tensor(MG2[:, db, :], tp2[4][:, 0:256], tp2[4][:, 256:512], ALU.add), t_pt_read)
        t = wout(a["wo2"].rearrange("(k p) n -> p k n", p=128), XX, lambda k: MG2[:, k, :], t_mg, None)
        sp = stream(a["pT"].rearrange("(k p) t -> p k t", p=128), [2, 256])
        sw = stream(a["wpp"].rearrange("(k p) n -> p k n", p=128), [2, 1024])
        pw = [sp.t, sw.t]
        t_h3 = norm(XX, HN, D, t, lambda k: vc_("nple", k), None, SQ3, rs3, 4, PE.last())
        wpg = a["wpg"].rearrange("(k p) n -> p k n", p=128)
        for c in range(4):
            b = 4 + c % 2
            for j in range(2):
                db = 2 * c + j
                tok = projT(sw.v, sw, slice(128 * db, 128 * db + 128), lambda k: sp.v[:, k, :], 256, B[b][:, 256 * j:256 * j + 256],
                            [pw, free[b]], kn=2)
            s = wslot(wpg, 256 * c)
            b1 = nextbank()
            for j in range(2):
                tok = projT(s.v, s, slice(128 * j, 128 * j + 128), Hn, 256, B[b1][:, 256 * j:256 * j + 256], [s.t, t_h3, free[b1]])
            done(s, tok)
            sg = tp2[c % 2]
            t, free[b1] = sigmoid(sg, B[b1], tok, V.last())
            V(lambda e, sg=sg, b=b: e.tensor_tensor(sg, sg, B[b], ALU.mult), t)
            free[b] = V.last()
            t = V(lambda e, sg=sg, c=c: e.tensor_tensor(pair(XX, c), pair(XX, c), sg, ALU.add))
        done(sp, PE.last())
        done(sw, PE.last())
        FINAL = MG2
        norm(XX, MG2, D, t, lambda k: vc_("nfin", k), None, SQ3, rs3, 4, PE.last())

        finish(FINAL)


def pack(inp):
    f = lambda x: np.ascontiguousarray(np.asarray(x)).astype(np.float32, copy=False)
    col = lambda x: np.asarray(x).reshape(-1, 128).T
    c2 = np.stack([np.asarray(inp["c"]).reshape(8, 128), np.asarray(inp["c_ctx"]).reshape(8, 128)], 1)
    parts = [c2.reshape(16, 128).T, col(inp["ada_b"]), col(inp["norm_mix_w"]), col(inp["norm_ffn_w"]),
             col(inp["hgrn_lb_logits"]), col(inp["hgrn_norm_w"]), col(inp["sgu_norm_w"]), col(inp["final_norm_w"]),
             col(inp["norm_mix_g_2"]), col(inp["b_merge_2"]), col(inp["b_gk_2"]), col(inp["gla_norm_g_2"]),
             col(inp["conv_w_2"]), col(inp["norm_ple_g_2"]), col(inp["norm_final_g_2"]),
             np.full((128, 1), EPS, np.float32)]
    vec = np.concatenate(parts, 1)
    assert vec.shape == (128, VN)
    i = np.arange(128)
    masks = np.stack([(i[:, None] // (2 * s) == i[None, :] // (2 * s)) for s in (64, 64, 32, 16, 8, 4, 2, 1)], 1)
    leaf = (i[:, None] // 64 == i[None, :] // 64) & (i[:, None] <= i[None, :])
    masks = np.concatenate([masks[:, 1:], np.eye(128, dtype=bool)[:, None, :], leaf[:, None, :]], 1).astype(np.float32)
    return dict(
        vec=f(vec), msk=np.ascontiguousarray(masks.reshape(128, 1152)), ident=np.eye(128, dtype=np.float32),
        iota=np.tile(np.arange(1, 33, dtype=np.float32), (128, 1)),
        x=f(inp["x"][0].T), ctx=f(inp["ctx"][0].T), ada_w=f(inp["ada_w"][0]), w_in=f(inp["w_in"][0]),
        wst=f(np.asarray(inp["sgu_w"])[0].transpose(0, 2, 1)), sgu_b=f(inp["sgu_b"][0]),
        w_branch_a=f(inp["w_branch_a"][0]), w_branch_b=f(inp["w_branch_b"][0]), w_out=f(inp["w_out"][0]),
        router_w=f(inp["router_w"][0]), wg=f(inp["expert_w_gate"][0]), wu=f(inp["expert_w_up"][0]),
        wd=f(inp["expert_w_down"][0]),
        w_in2=f(inp["w_in_2"][0]), w_gk2=f(inp["w_gk2_2"][0]), wa2=f(inp["w_branch_a_2"][0]),
        wc2=f(inp["w_branch_c_2"][0]), wo2=f(inp["w_out_2"][0]), wpg=f(inp["w_ple_gate_2"][0]),
        wpp=f(inp["w_ple_proj_2"][0]), pT=f(np.asarray(inp["p_2"])[0, 0].T),
    )


def kernel(**inputs):
    import concourse.bacc as _bacc
    from concourse.bass_utils import run_bass_kernel_spmd as _run

    nc = _bacc.Bacc("TRN2", target_bir_lowering=False, num_devices=1)
    arrays = {f"in_{k}": v for k, v in pack(inputs).items()}
    aps = {k[3:]: nc.dram_tensor(k, v.shape, mybir.dt.from_np(v.dtype), kind="ExternalInput").ap() for k, v in arrays.items()}
    out = nc.dram_tensor("out_dram", (D, T), F32, kind="ExternalOutput").ap()
    program(nc, aps, out)
    r = _run(nc, [arrays], core_ids=[0])
    return np.ascontiguousarray(r.results[0]["out_dram"].T).reshape(1, T, D)
```

```python
from contextlib import ExitStack

import numpy as np

import concourse.bass as bass
from concourse import mybir

F32 = mybir.dt.float32
U8 = mybir.dt.uint8
FR = mybir.dt.float32r
ALU = mybir.AluOpType
ACT = mybir.ActivationFunctionType
AX = mybir.AxisListType.X

T = 256
D = 1024
NE = 16
EPS = 1e-6
SLOT = 2048
BASE_SLOTS = 5
MORE_SLOTS = 11
EARLY = 6
WINDOW, WINDOWED = 4, 14
GELU_C = 2.0 * 0.7978845608028654

VEC = dict(c=16, ada_b=48, nmix=8, nffn=8, lb=16, hgn=4, sgn=4, fnw=8, nm2=8, bm2=16, bgk=4, gng=2,
           cw=24, nple=8, nfin=8, eps=1)
VOFF, VN = {}, 0
for _k, _n in VEC.items():
    VOFF[_k] = VN
    VN += _n


class Queue:

    def __init__(self, sem, linked):
        self.sem, self.linked, self.n, self.ops, self.seen = sem, linked, 0, [], {}
        self.value = {}

    def __call__(self, fn, *waits, link=True):
        waits = list(waits)
        if self.linked and link and self.n:
            waits.append((self, self.n))
        self.ops.append((news(self.seen, waits), fn))
        self.n += 1
        return (self, self.n)

    def last(self):
        return (self, self.n)

    def emit(self, eng):
        for n, (need, fn) in enumerate(self.ops):
            for w in need:
                await_(eng, w)
            ins = fn(eng)
            if n + 1 in self.value:
                ins.then_inc(self.sem, 1)


def news(seen, waits):
    need = []
    for w in flat(waits):
        if seen.get(id(w[0]), 0) < w[1]:
            seen[id(w[0])] = w[1]
            need.append(w)
    return need


def await_(eng, w):
    src, n = w
    if isinstance(src, Queue):
        eng.wait_ge(src.sem, src.value[n])
    else:
        eng.wait_ge(src, n)


def number(queues, needs):
    used = {}
    for src, n in needs + [w for q in queues for need, _ in q.ops for w in need]:
        if isinstance(src, Queue):
            used.setdefault(id(src), set()).add(n)
    for q in queues:
        q.value = {n: i + 1 for i, n in enumerate(sorted(used.get(id(q), ())))}


def flat(x):
    if x is None:
        return []
    if isinstance(x, list):
        return [z for y in x for z in flat(y)]
    return [x]


def program(nc, a, out):
    ctx = ExitStack()
    with ctx:
        def sem(name):
            return ctx.enter_context(nc.semaphore(name))

        TOT, ZONE = 52992, BASE_SLOTS * SLOT + 3408
        M = ctx.enter_context(nc.sbuf_tensor("M", [128, ZONE], F32))
        Z = ctx.enter_context(nc.sbuf_tensor("Z", [128, TOT - ZONE], F32))
        m_at = nc.sbuf_base - 4 * TOT
        B = [ctx.enter_context(nc.psum_tensor(f"B{i}", [128, 512], F32))[:, :] for i in range(8)]

        PE = Queue(sem("s_pe"), False)
        V = Queue(sem("s_dve"), True)
        A = Queue(sem("s_act"), True)
        G = Queue(sem("s_pool"), True)
        SP = []

        pos = [0]

        def new(n, at=None):
            o = pos[0] if at is None else at[0]
            (pos if at is None else at)[0] = o + (n + 7) // 8 * 8
            assert o + n <= TOT, (o, n)
            return M[:, o:o + n] if o < ZONE else Z[:, o - ZONE:o - ZONE + n]

        rounded = [0]

        def R(ap, n):
            rounded[0] += 1
            first = ap.offset + (0 if ap.tensor.name == "M" else ZONE)
            t = nc.alloc_sbuf_tensor_at(f"R{rounded[0]}", [128, n], FR, offset=m_at + 4 * first)
            return t[:, :]

        slots = [new(SLOT) for _ in range(BASE_SLOTS)]
        XX = new(2048).rearrange("p (k t) -> p k t", k=8)
        vec = new(VN)
        ones = new(128)
        ident = new(128)
        iot = new(32)
        cms = new(288)
        msk = cms.bitcast(U8).rearrange("p (s i) -> p s i", s=9)
        csil = new(256).rearrange("p (k r) -> p k r", k=8)
        mod = new(96).rearrange("p (m r) -> p m r", r=2)
        swm = new(16).rearrange("p (k r) -> p k r", r=2)
        swf = new(8)
        lbv = new(32)
        ctmp = new(64)
        wr = new(128).rearrange("p (k n) -> p k n", k=8)
        zone = pos[0]
        assert zone == ZONE
        z1 = [zone]
        more = [new(SLOT, z1) for _ in range(MORE_SLOTS)]
        late = z1[0]
        z1 = [zone]
        h4 = lambda: new(1024, z1).rearrange("p (h t) -> p h t", h=4)
        HTh0 = new(4096, z1)
        PT = new(2048, z1).rearrange("p (j h i) -> p j h i", j=2, h=4)
        kb, qT, EK, EQ = h4(), h4(), h4(), h4()
        vx = new(1024, z1).rearrange("p (i n) -> p i n", i=2)
        St = new(1024, z1).rearrange("p (d n) -> p d n", d=2)
        XC = new(2048, z1).rearrange("p (k t) -> p k t", k=8)
        HT0 = new(4096, z1)
        HT = HT0.rearrange("p (k t) -> p k t", k=8)
        HTl = R(HT0, 4096).rearrange("p (k t) -> p k t", k=8)
        HTh = R(HTh0, 4096).rearrange("p (k t) -> p k t", k=8)
        WH = [R(new(2048, z1), 2048) for _ in range(3)]
        vc = new(1024, z1).rearrange("p (i n) -> p i n", i=2)
        wtok = new(2048, z1).rearrange("p (i n) -> p i n", i=2)
        bf, bb, kf, MK, MQ = h4(), h4(), h4(), h4(), h4()
        oT = kf
        gT = vc.rearrange("p i n -> p (i n)").rearrange("p (h t) -> p h t", h=4)
        uT = new(1024, z1).rearrange("p (h t) -> p h t", h=4)
        svt = new(1024, z1).rearrange("p (i n) -> p i n", i=2)
        tmp = [new(512, z1) for _ in range(6)]
        wst = new(512, z1).rearrange("p (g t) -> p g t", g=4)
        bsb = new(512, z1).rearrange("p (g t) -> p g t", g=4)
        wctx, SA = XC, XC
        SB = wtok.rearrange("p i n -> p (i n)").rearrange("p (k t) -> p k t", k=8)
        r4 = lambda x: x.rearrange("p (h t) -> p h t", h=4)
        oTh, oTl, uTh, uTl = (r4(R(x, 1024)) for x in (bf, oT, bb, uT))
        MG, MGl = HT[:, :, 0:256], R(HT0, 4096).rearrange("p (k t) -> p k t", k=8)[:, :, 0:256]
        MGh = R(MK, 2048).rearrange("p (k t) -> p k t", k=8)

        def vc_(name, i=0, n=1):
            return vec[:, VOFF[name] + i:VOFF[name] + i + n]

        def load(dst, src, name, first=False):
            s = sem(name)
            (early if first else second).append((dst, src, s))
            return (s, 16)

        early, second = [], []
        t_vec = load(vec, a["vec"], "l_vec", True)
        t_x = load(XX, a["x"].rearrange("(k p) t -> p k t", p=128), "l_x", True)
        t_c = load(XC, a["ctx"].rearrange("(k p) t -> p k t", p=128), "l_c", True)
        t_mf = load(PT.rearrange("p j h i -> p (j h i)")[:, 0:1152], a["msk"], "l_msk")
        t_id = load(ident, a["ident"], "l_id", True)
        t_iot = load(iot, a["iota"], "l_iot")
        t_wst = load(wst, a["wst"].rearrange("g s t -> s g t"), "l_wst")
        t_bsb = load(bsb, a["sgu_b"].rearrange("(o g) t -> o (g t)", o=1).broadcast_to([128, 512]), "l_bsb")
        t_wr = load(wr, a["router_w"].rearrange("(k p) n -> p k n", p=128), "l_wr")

        ring = list(range(BASE_SLOTS))
        at = [0]
        ssem = [sem(f"r{i}") for i in range(BASE_SLOTS + MORE_SLOTS + 6)]
        scount = [0] * (BASE_SLOTS + MORE_SLOTS + 6)
        aux = [Z[:, o:o + SLOT] for o in (EK.offset, MK.offset, uT.offset, PT.offset, HTh0.offset, HTh0.offset + SLOT)]
        allslots = slots + more + aux
        last_done = {}

        class Slot:
            pass

        def stream(src, shape, parts=128, i=None):
            if i is None:
                i = ring[at[0] % len(ring)]
                at[0] += 1
            s = Slot()
            s.i = i
            n = int(np.prod(shape))
            view = allslots[i][0:parts, 0:n]
            if len(shape) == 2:
                view = view.rearrange("p (a b) -> p a b", a=shape[0])
            elif len(shape) == 3:
                view = view.rearrange("p (a b c) -> p a b c", a=shape[0], b=shape[1])
            s.v = view
            scount[i] += 16
            s.t = (ssem[i], scount[i])
            s.prev = last_done.get(i)
            last_done[i] = s
            s.free, s.wh = None, None
            SP.append((s, view, src))
            return s

        def done(s, tok):
            s.free = tok
            if s.wh is not None:
                wh_free[s.wh] = tok
                held[0] -= 1

        plan, ready, wh_free, wh_n, held = [], [], [None] * 3, [0], [0]

        def ahead():
            if not plan or plan[0] is None or len(ready) + held[0] > 2:
                return
            src, shape = plan.pop(0)
            s = stream(src, shape)
            n = int(np.prod(shape))
            s.wh = wh_n[0] % 3
            wh_n[0] += 1
            flat_ = slots[s.i][:, 0:n]
            hi, lo = whs[0][s.wh][:, 0:n], slotR[s.i][:, 0:n]
            t = A(lambda e: e.activation(hi, flat_, ACT.Copy), s.t, wh_free[s.wh])
            s.t = G(lambda e: e.tensor_tensor(lo, flat_, hi.bitcast(F32), ALU.subtract), t, s.t)
            shaped = lambda x: x.rearrange("p (k n) -> p k n", k=shape[0])
            s.h, s.l = shaped(hi), shaped(lo)
            ready.append(s)

        def take():
            if not ready:
                if plan[0] is None:
                    plan.pop(0)
                ahead()
            held[0] += 1
            return ready.pop(0)

        slotR = [R(x, SLOT) for x in slots]
        whs = [WH]

        def mm3(out_, wh, wl, ah, al, kn, waits, w_first=True, per_k=None):
            for k in range(kn):
                for j, (w, x) in enumerate(((wh, ah), (wh, al), (wl, ah))):
                    lhs, rhs = (w, x) if w_first else (x, w)
                    tok = PE(lambda e, lhs=lhs, rhs=rhs, k=k, j=j: e.matmul(out_, lhs(k), rhs(k), start=k == 0 and j == 0,
                                                                          stop=k == kn - 1 and j == 2),
                             *((waits if k == 0 else []) + ([per_k[k]] if per_k else []) if j == 0 else []))
            return tok

        def split_a(hi, lo, x, *waits):
            t = A(lambda e: e.activation(hi, x, ACT.Copy), *waits)
            return V(lambda e: e.tensor_tensor(lo, x, hi.bitcast(F32), ALU.subtract), t)

        def finish(final, t_out):
            outs = []
            everything = [q.last() for q in (PE, V, A, G) if q.n] + [(s, 16) for _, _, s in early + second]
            for c in range(4):
                outs.append((out.rearrange("(k p) t -> p k t", p=128)[:, 2 * c:2 * c + 2, :], final[:, 2 * c:2 * c + 2, :]))
            s_out = sem("s_out")
            block = ctx.enter_context(nc.Block())

            seen, loads = {}, []
            for sl_, view, src in SP:
                n = len(loads)
                window = SP[n - WINDOW][0].t if WINDOW <= n < WINDOWED else None
                need = news(seen, [sl_.prev.free if sl_.prev is not None else None, window])
                loads.append((need, view, src, ssem[sl_.i]))
            loads[28:28] = [([], dst, src, s) for dst, src, s in second[1:]]
            loads[9:9] = [([], dst, src, s) for dst, src, s in second[:1]]
            number([PE, V, A, G], [w for need, *_ in loads for w in need] + everything + flat(t_out))

            @block.sync
            def _(eng):
                for need, view, src, s in loads:
                    for w in need:
                        await_(eng, w)
                    eng.dma_start(view, src).then_inc(s, 16)
                for c, (dst, src) in enumerate(outs):
                    await_(eng, t_out[2 * c + 1])
                    eng.dma_start(dst, src).then_inc(s_out, 16)
                for w in everything:
                    await_(eng, w)
                eng.wait_ge(s_out, 16 * len(outs))

            @block.scalar
            def _(eng):
                for dst, src, s in early:
                    eng.dma_start(dst, src).then_inc(s, 16)
                eng.preload_act_table_set("natural_log_exp_and_others")
                A.emit(eng)

            @block.vector
            def _(eng):
                V.emit(eng)

            @block.gpsimd
            def _(eng):
                G.emit(eng)

            @block.tensor
            def _(eng):
                PE.emit(eng)

        g0 = G(lambda e: e.memset(ones, 1.0))
        g1 = G(lambda e: e.memset(csil.rearrange("p k r -> p (k r)"), 0.0))
        cv = vc_("c", 0, 16)
        a0 = A(lambda e: e.activation(ctmp[:, 0:16], cv, ACT.Exp, scale=-1.0), t_vec)
        V(lambda e: e.tensor_scalar(ctmp[:, 16:32], ctmp[:, 0:16], 1.0, None, ALU.add), a0)
        V(lambda e: e.reciprocal(ctmp[:, 32:48], ctmp[:, 16:32]))
        t_csil = V(lambda e: e.tensor_tensor(csil[:, :, 0:2], cv.rearrange("p (k r) -> p k r", r=2),
                                             ctmp[:, 32:48].rearrange("p (k r) -> p k r", r=2), ALU.mult),
                   t_vec, g1)
        lg = vc_("lb", 0, 16).rearrange("p (d l h) -> p d l h", d=2, l=2)
        lt = ctmp[:, 0:16].rearrange("p (d l h) -> p d l h", d=2, l=2)
        mx = ctmp[:, 16:24].rearrange("p (d h) -> p d h", d=2)
        V(lambda e: e.tensor_tensor(mx, lg[:, :, 0, :], lg[:, :, 1, :], ALU.max))
        V(lambda e: e.tensor_tensor(lt[:, :, 0, :], lg[:, :, 0, :], mx, ALU.subtract))
        v0 = V(lambda e: e.tensor_tensor(lt[:, :, 1, :], lg[:, :, 1, :], mx, ALU.subtract))
        a1 = A(lambda e: e.activation(ctmp[:, 24:40], ctmp[:, 0:16], ACT.Exp), v0)
        le = ctmp[:, 24:40].rearrange("p (d l h) -> p d l h", d=2, l=2)
        V(lambda e: e.tensor_tensor(mx, le[:, :, 0, :], le[:, :, 1, :], ALU.add), a1)
        V(lambda e: e.reciprocal(ctmp[:, 40:48], ctmp[:, 16:24]))
        V(lambda e: e.tensor_tensor(lbv[:, 0:8].rearrange("p (d h) -> p d h", d=2), le[:, :, 0, :],
                                    ctmp[:, 40:48].rearrange("p (d h) -> p d h", d=2), ALU.mult))
        V(lambda e: e.tensor_scalar(lbv[:, 8:16], lbv[:, 0:8], -1.0, 1.0, ALU.mult, ALU.add))
        lb = lambda d, h: lbv[:, 4 * d + h:4 * d + h + 1]
        olb = lambda d, h: lbv[:, 8 + 4 * d + h:9 + 4 * d + h]

        def rstd(dst, src, n, *waits):
            t = A(lambda e: e.activation(dst, src, ACT.Ln, bias=vc_("eps"), scale=1.0 / n), *waits)
            return A(lambda e: e.activation(dst, dst, ACT.Exp, scale=-0.5))

        free = {i: None for i in range(8)}

        SQ = [EK, EQ, MK, MQ]
        rs = tmp[0]
        s_all = []
        for which, (src, tsrc) in enumerate(((XC, t_c), (XX, t_x))):
            part = tmp[1][:, 256 * which:256 * which + 256]
            toks = []
            for h in range(2):
                sq = SQ[2 * which + h]
                toks.append(A(lambda e, sq=sq, src=src, h=h: e.activation(sq, src[:, 4 * h:4 * h + 4, :], ACT.Square), tsrc))
            lo, hi = SQ[2 * which], SQ[2 * which + 1]
            V(lambda e, lo=lo, hi=hi: e.tensor_tensor(lo, lo, hi, ALU.add), toks)
            V(lambda e, lo=lo: e.tensor_tensor(lo[:, 0:2, :], lo[:, 0:2, :], lo[:, 2:4, :], ALU.add))
            s_all.append(V(lambda e, lo=lo, part=part: e.tensor_tensor(part, lo[:, 0, :], lo[:, 1, :], ALU.add)))
        t_mod = {}

        def ada(q, k, s, row):
            for j in range(4):
                tok = PE(lambda e, j=j: e.matmul(B[0][32 * j:32 * j + 32, :], csil[:, k, :], s.v[:, 512 * j:512 * j + 512],
                                                 start=k == 0, stop=k == 7), s.t, t_csil, free[0])
            done(s, tok)
            if k < 7:
                return
            vt = free[0] = V(lambda e: e.tensor_copy(row, B[0]), tok)
            for c in range(4):
                tok = PE(lambda e, c=c: e.transpose(B[1][:, 128 * c:128 * c + 128], row[:, 128 * c:128 * c + 128], ident),
                         vt, t_id, free[1])
            o = mod[:, 16 * q:16 * q + 16, :].rearrange("p (j c) r -> p j c r", j=4)
            i0 = B[1][:, :].rearrange("p (c j r) -> p j c r", c=4, j=4)
            bias = vc_("ada_b", 16 * q, 16).rearrange("p (j c o) -> p j c o", j=4, o=1).broadcast_to([128, 4, 4, 2])
            for r in range(2):
                free[1] = V(lambda e, r=r: e.tensor_tensor(o[:, :, :, r], i0[:, :, :, r], bias[:, :, :, r], ALU.add), tok)
            t_mod[q] = free[1]

        ada_src = lambda q, k: a["ada_w"][k * 128:(k + 1) * 128, q * 2048:(q + 1) * 2048]

        def scaled():
            p0 = PE(lambda e: e.matmul(B[7], ones, tmp[1], start=True, stop=True), s_all, g0)
            t_rs = free[7] = rstd(rs, B[7], D, p0)
            for k in range(8):
                V(lambda e, k=k: e.tensor_tensor(HT[:, k, 0:256], XC[:, k, :], rs[:, 0:256], ALU.mult), t_rs)
                t_xn.append(V(lambda e, k=k: e.tensor_tensor(HT[:, k, 256:512], XX[:, k, :], rs[:, 256:512], ALU.mult)))

        t_xn = []
        QO, FO, BO, VO, GO, UO, SO, AO, CO = 0, 512, 1024, 1536, 2048, 2560, 3072, 3584, 4608
        win = a["w_in"].rearrange("(k p) n -> p k n", p=128)

        def wants(src, c0, n=256, kn=8):
            plan.append((src[:, :, c0:c0 + n], [kn, n]))

        for off, n in ((FO, 2), (BO, 2), (QO, 2), (VO, 2), (SO, 2), (UO, 2), (GO, 2), (AO, 4), (CO, 4)):
            for hh in range(n):
                wants(win, off + 256 * hh)
        wa = a["w_branch_a"].rearrange("(k p) n -> p k n", p=128)
        wb = a["w_branch_b"].rearrange("(k p) n -> p k n", p=128)
        wo = a["w_out"].rearrange("(k p) n -> p k n", p=128)
        for c in range(2):
            wants(wa, 512 * c, 512, 4)
            wants(wb, 512 * c, 512, 4)
        for c in range(4):
            wants(wo, 256 * c)

        AUX = BASE_SLOTS + MORE_SLOTS
        sl = [stream(ada_src(0, k), [2048], i=(None if k < 4 else AUX + (2, 4, 5)[k - 4])) for k in range(7)]
        for k in range(8):
            if k == 7:
                ahead()
                sl.append(stream(ada_src(0, 7), [2048]))
            ada(0, k, sl[k], tmp[2])
            if k == 3:
                scaled()
        nb = vc_("nmix", 0, 8).rearrange("p (k o) -> p k o", o=1).broadcast_to([128, 8, 2])
        for r in range(2):
            t_sw = V(lambda e, r=r: e.scalar_tensor_tensor(swm[:, :, r], mod[:, 8:16, r], 1.0, nb[:, :, r],
                                                           ALU.add, ALU.mult))
        bankno = [0]

        def nextbank():
            bankno[0] += 1
            return (2, 3, 6, 7)[bankno[0] % 4]

        def projT(s, cols, ah, al, bank, waits, kn=8, per_k=None):
            return mm3(bank, lambda k: s.h[:, k, cols], lambda k: s.l[:, k, cols], ah, al, kn, [s.t] + waits, per_k=per_k)

        Hx = (lambda k: HTh[:, k, 256:512], lambda k: HTl[:, k, 256:512])
        Hall = (lambda k: HTh[:, k, :], lambda k: HTl[:, k, :])
        t_msk = G(lambda e: e.tensor_copy(cms.bitcast(U8), PT.rearrange("p j h i -> p (j h i)")[:, 0:1152]), t_mf)
        rest, later = [(q, k) for q in (1, 2) for k in range(8)], []
        for i in range(4):
            s = Slot()
            s.free = [s_all, t_msk, last_done[AUX + i].free if AUX + i in last_done else None]
            last_done[AUX + i] = s

        def load_rest():
            if rest:
                q, k = rest.pop(0)
                later.append((q, k, stream(ada_src(q, k), [2048], i=BASE_SLOTS + MORE_SLOTS + (8 * q + k) % 4)))

        def modulate():
            if later:
                q, k, s = later.pop(0)
                ada(q, k, s, vx[:, 0, :])
                load_rest()

        t_h, his = [], []
        for k in range(9):
            if k < 8:
                hc, hx = HT[:, k, 0:256], HT[:, k, 256:512]
                t = V(lambda e, k=k, hc=hc: e.tensor_scalar(hc, hc, swm[:, k, 1:2], mod[:, k, 1:2], ALU.mult, ALU.add))
                A(lambda e, k=k, hx=hx: e.activation(hx, hx, ACT.Identity, bias=mod[:, k, 0:1], scale=swm[:, k, 0:1]), t_sw, t_xn)
                his.append(A(lambda e, k=k: e.activation(HTh[:, k, :], HT[:, k, :], ACT.Copy), t))
            if k:
                t_h.append(V(lambda e, k=k - 1: e.tensor_tensor(HTl[:, k, :], HT[:, k, :], HTh[:, k, :].bitcast(F32), ALU.subtract),
                             his[k - 1]))
            if k in (4, 8):
                ahead()
                load_rest()
                load_rest()

        def sigmoid(dst, src, *waits):
            w = V(lambda e: e.tensor_scalar(dst, src, -43.0, None, ALU.max), *waits)
            A(lambda e: e.activation(dst, dst, ACT.Exp, scale=-1.0), w)
            A(lambda e: e.activation(dst, dst, ACT.Ln, bias=ones[:, 0:1]))
            return A(lambda e: e.activation(dst, dst, ACT.Exp, scale=-1.0)), w

        tk = {}
        for d in range(2):
            for hh in range(2):
                s = take()
                for j in range(2):
                    h = 2 * hh + j
                    b = nextbank()
                    ps = B[b]
                    tok = projT(s, slice(128 * j, 128 * j + 128), *Hall, ps, [free[b]], per_k=t_h)
                    if j:
                        done(s, tok)
                    ahead()
                    if (d, h) != (0, 0):
                        modulate()
                        modulate()
                    f, lf, cu = tmp[(h % 2) * 3], tmp[(h % 2) * 3 + 1], tmp[(h % 2) * 3 + 2]
                    t0, free[b] = sigmoid(f, ps[:, :], tok, tk.get(("f", h % 2)))
                    V(lambda e, f=f, d=d, h=h: e.tensor_scalar(f, f, olb(d, h), lb(d, h), ALU.mult, ALU.add), t0)
                    t1 = V.last()
                    ta = A(lambda e, f=f, lf=lf: e.activation(lf, f, ACT.Ln), t1)
                    kx, bx = (kf, kb)[d], (bf, bb)[d]
                    V(lambda e, f=f, kx=kx, h=h: e.tensor_scalar(kx[:, h, :], f[:, 256:512], -1.0, 1.0, ALU.mult, ALU.add))
                    kc = cu[:, 256:512]
                    V(lambda e, f=f, kc=kc: e.tensor_scalar(kc, f[:, 0:256], -1.0, 1.0, ALU.mult, ALU.add))
                    st = -1 if d else 1
                    onr = ones[:, 0:1].broadcast_to([128, 256])
                    V(lambda e, bx=bx, h=h, lf=lf, st=st, onr=onr: e.tensor_tensor_scan(
                        bx[:, h, ::st], onr, lf[:, 256:512][:, ::st], 0.0, ALU.mult, ALU.add), ta, g0)
                    cc = cu[:, 0:256]
                    t2 = V(lambda e, cc=cc, lf=lf, st=st, onr=onr: e.tensor_tensor_scan(
                        cc[:, ::st], onr, lf[:, 0:256][:, ::st], 0.0, ALU.mult, ALU.add))
                    lastc = cc[:, 0:1] if d else cc[:, 255:256]
                    t3 = A(lambda e, f=f, cc=cc, lastc=lastc: e.activation(f[:, 0:256], cc, ACT.Exp, bias=lastc, scale=-1.0), t2)
                    tk["f", h % 2] = t3
                    tw = V(lambda e, f=f, kc=kc, d=d, h=h: e.tensor_tensor(wctx[:, 4 * d + h, :], kc, f[:, 0:256], ALU.mult), t3)
                    tk["w", d, h] = tw
                    tk["f", h % 2] = [t3, tw]
            tk["b", d] = tw

        t_v = []

        def p_v():
            s = take()
            hh = len(t_v)
            for i in range(4):
                b = nextbank()
                tk_ = slice(128 * i, 128 * i + 128)
                tok = mm3(B[b][:, 0:256], lambda k: s.h[:, k, :], lambda k: s.l[:, k, :], lambda k, tk_=tk_: HTh[:, k, tk_],
                          lambda k, tk_=tk_: HTl[:, k, tk_], 8, [s.t, free[b]], w_first=False)
                if i == 0:
                    ahead()
                dst = (vc, vx)[i // 2][:, i % 2, 256 * hh:256 * hh + 256]
                free[b] = A(lambda e, dst=dst, b=b: e.activation(dst, B[b][:, 0:256], ACT.Copy), tok)
            done(s, tok)
            t_v.append(free[b])

        for hh in range(2):
            s = take()
            b = nextbank()
            for j in range(2):
                tok = projT(s, slice(128 * j, 128 * j + 128), *Hx, B[b][:, 256 * j:256 * j + 256], [free[b]])
            done(s, tok)
            ahead()
            modulate()
            sg = tmp[hh]
            t0, _ = sigmoid(sg, B[b][:, :], tok, tk["f", 0], tk["f", 1])
            free[b] = V(lambda e, hh=hh, sg=sg, b=b: e.tensor_tensor(qT[:, 2 * hh:2 * hh + 2, :].rearrange("p h t -> p (h t)"),
                                                                    sg, B[b][:, :], ALU.mult), t0)
        t_q = free[b]

        t_S = []

        def states():
            tr = {}
            for d in range(2):
                for i in range(2):
                    b = 4 + i
                    for h in range(4):
                        tok = PE(lambda e, b=b, d=d, h=h, i=i: e.transpose(B[b][:, 128 * h:128 * h + 128],
                                                                          wctx[:, 4 * d + h, 128 * i:128 * i + 128], ident),
                                 tk["b", 1], t_id, free[b])
                    tr[d, i] = A(lambda e, b=b, d=d, i=i: e.activation(wtok[:, i, 512 * d:512 * d + 512], B[b][:, :], ACT.Copy), tok)
                    free[b] = tr[d, i]
            for d in range(2):
                b = 6 + d
                for h in range(4):
                    for i in range(2):
                        tok = PE(lambda e, b=b, d=d, h=h, i=i: e.matmul(B[b][:, 128 * h:128 * h + 128],
                                                                       wtok[:, i, 512 * d + 128 * h:512 * d + 128 * h + 128],
                                                                       vc[:, i, 128 * h:128 * h + 128], start=i == 0, stop=i == 1),
                                 tr[d, 1], t_v, free[b])
                tS = A(lambda e, b=b, d=d: e.activation(St[:, d, :], B[b][:, :], ACT.Copy), tok)
                free[b] = tS
            t_S.append(tS)

        def split(x, s):
            return x.rearrange("p h (n w t) -> p (h n) w t", w=2, t=s)

        t_lv = None
        levels = [128, 64, 32, 16, 8, 4, 2, 1, 0]

        sets = [(EK, EQ), (MK, MQ)]
        t_el, pe_lv = {}, {}

        def elements(li):
            s = levels[li]
            K0, Q0 = sets[li % 2]
            wk = pe_lv.get(li - 2)
            if s == 0:
                t_el[li] = V(lambda e: e.tensor_tensor(K0, kf, kb, ALU.add), wk)
                return
            n = 1024 // (2 * s)
            F_, B_ = split(bf, s), split(bb, s)
            K_, Q_ = split(K0, s), split(Q0, s)
            rf = F_[:, :, 0, s - 1:s].broadcast_to([128, n, s])
            rb = B_[:, :, 1, 0:1].broadcast_to([128, n, s])
            V(lambda e: e.tensor_tensor(K_[:, :, 0, :], rf, F_[:, :, 0, :], ALU.subtract), tk["b", 1], wk)
            t1 = V(lambda e: e.tensor_tensor(K_[:, :, 1, :], rb, B_[:, :, 1, :], ALU.subtract))
            G(lambda e: e.tensor_tensor(Q_[:, :, 1, :], F_[:, :, 1, :], rf, ALU.subtract), tk["b", 1], wk)
            t2 = G(lambda e: e.tensor_tensor(Q_[:, :, 0, :], B_[:, :, 0, :], rb, ALU.subtract))
            ta = A(lambda e: e.activation(K0, K0, ACT.Exp), t1)
            tb = A(lambda e: e.activation(Q0, Q0, ACT.Exp), t2)
            V(lambda e: e.tensor_tensor(K_[:, :, 0, :], split(kf, s)[:, :, 0, :], K_[:, :, 0, :], ALU.mult), ta)
            t1 = V(lambda e: e.tensor_tensor(K_[:, :, 1, :], split(kb, s)[:, :, 1, :], K_[:, :, 1, :], ALU.mult))
            t2 = V(lambda e: e.tensor_tensor(Q0, qT, Q0, ALU.mult), tb, t_q)
            t_el[li] = [t1, t2]

        def scores(li):
            nonlocal t_lv
            s = levels[li]
            K0, Q0 = sets[li % 2]
            if s == 0:
                Q0 = qT
            for j in range(2):
                i = 1 - j if s == 128 else j
                for h in range(4):
                    tok = PE(lambda e, h=h, i=i, j=j: e.matmul(B[4 + j][:, 128 * h:128 * h + 128], K0[:, h, 128 * j:128 * j + 128],
                                                               Q0[:, h, 128 * i:128 * i + 128], start=True, stop=True),
                             t_el[li], free[4 + j])
                dst = PT[:, j, :, 128 * i:128 * i + 128]
                src = B[4 + j].rearrange("p (h i) -> p h i", h=4)
                if s >= 64:
                    free[4 + j] = V(lambda e, dst=dst, src=src: e.tensor_copy(dst, src), tok, t_msk)
                else:
                    m = msk[:, li - 1, :].rearrange("p (o i) -> p o i", o=1).broadcast_to([128, 4, 128])
                    free[4 + j] = V(lambda e, dst=dst, src=src, m=m: e.copy_predicated(dst, m, src), tok)
            pe_lv[li] = tok
            t_lv = free[5]

        pending, flip = [], [0]

        def defer(b, f):
            pending.append((b, f))

        def flush():
            while pending:
                b, f = pending.pop(0)
                free[b] = f()

        def gelu(dst, ps, n, b, *waits):
            flip[0] ^= 2
            x1, x2 = tmp[flip[0]][:, 0:n], tmp[flip[0] + 1][:, 0:n]
            t = A(lambda e: e.activation(x1, ps, ACT.Square), *waits, V.last())
            V(lambda e: e.tensor_scalar(x1, x1, 0.044715, 1.0, ALU.mult, ALU.add), t)
            V(lambda e: e.tensor_tensor(x2, x1, ps, ALU.mult))
            t = V(lambda e: e.tensor_scalar(x2, x2, -43.0 / GELU_C, None, ALU.max))
            A(lambda e: e.activation(x2, x2, ACT.Exp, scale=-GELU_C), t)
            A(lambda e: e.activation(x2, x2, ACT.Ln, bias=ones[:, 0:1]))
            t = A(lambda e: e.activation(x2, x2, ACT.Exp, scale=-1.0))
            defer(b, lambda: V(lambda e: e.tensor_tensor(dst, x2, ps, ALU.mult), t))

        def p_sv(hh):
            s = take()
            for i in range(2):
                b = nextbank()
                tk_ = slice(256 + 128 * i, 384 + 128 * i)
                tok = mm3(B[b][:, 0:256], lambda k: s.h[:, k, :], lambda k: s.l[:, k, :], lambda k, tk_=tk_: HTh[:, k, tk_],
                          lambda k, tk_=tk_: HTl[:, k, tk_], 8, [s.t, free[b]], w_first=False)
                if i == 0:
                    ahead()
                gelu(svt[:, i, 256 * hh:256 * hh + 256], B[b][:, 0:256], 256, b, tok)
            done(s, tok)

        def p_two(off, hh, fn):
            s = take()
            b = nextbank()
            for j in range(2):
                tok = projT(s, slice(128 * j, 128 * j + 128), *Hx, B[b][:, 256 * j:256 * j + 256], [free[b]])
            done(s, tok)
            ahead()
            fn(hh, B[b][:, :], tok, b)

        def e_u(hh, ps, tok, b):
            gelu(uT[:, 2 * hh:2 * hh + 2, :].rearrange("p h t -> p (h t)"), ps, 512, b, tok)

        def e_g(hh, ps, tok, b):
            dst = gT[:, 2 * hh:2 * hh + 2, :].rearrange("p h t -> p (h t)")
            t, _ = sigmoid(dst, ps, tok)
            defer(b, lambda: V(lambda e: e.tensor_tensor(dst, dst, ps, ALU.mult), t))

        def e_s(buf):
            def f(hh, ps, tok, b):
                dst = buf[:, 2 * hh:2 * hh + 2, :].rearrange("p h t -> p (h t)")
                t, free[b] = sigmoid(dst, ps, tok)
            return f

        work = [lambda: p_sv(0), lambda: p_sv(1), lambda: p_two(UO, 0, e_u), lambda: p_two(UO, 1, e_u),
                lambda: p_two(GO, 0, e_g), lambda: p_two(GO, 1, e_g)]
        work += [lambda i=i: p_two(AO, i, e_s(SA)) for i in range(4)] + [lambda i=i: p_two(CO, i, e_s(SB)) for i in range(4)]
        work = [p_v, lambda: (p_v(), states())] + work
        tq = []
        elements(0)
        for li in range(len(levels)):
            if li + 1 < len(levels):
                elements(li + 1)
            if levels[li] == 0:
                for bx, ex in ((bf, MK), (bb, MQ)):
                    t = A(lambda e, bx=bx, ex=ex: e.activation(ex, bx, ACT.Exp), pe_lv[li - 1], V.last())
                    tq.append(V(lambda e, ex=ex: e.tensor_tensor(ex, ex, qT, ALU.mult), t))
            flush()
            if work:
                work.pop(0)()
            scores(li)
        flush()

        t_o = []
        for h in range(4):
            b = 6 + h // 2
            po = B[b][:, 256 * (h % 2):256 * (h % 2) + 256]
            hs = slice(128 * h, 128 * h + 128)
            tok = PE(lambda e, po=po, h=h, hs=hs: e.matmul(po, St[:, 0, hs], MK[:, h, :], start=True, stop=False), t_S, tq, free[b])
            PE(lambda e, po=po, h=h, hs=hs: e.matmul(po, St[:, 1, hs], MQ[:, h, :], start=False, stop=False))
            PE(lambda e, po=po, h=h, hs=hs: e.matmul(po, vx[:, 0, hs], PT[:, 0, h, :], start=False, stop=False), t_lv)
            tok = PE(lambda e, po=po, h=h, hs=hs: e.matmul(po, vx[:, 1, hs], PT[:, 1, h, :], start=False, stop=True))
            if h % 2:
                ov = oT[:, h - 1:h + 1, :].rearrange("p h t -> p (h t)")
                t = V(lambda e, ov=ov, b=b: e.tensor_copy(ov, B[b][:, :]), tok)
                free[b] = t
                sq = tmp[2 + h // 2]
                ta = A(lambda e, ov=ov, sq=sq: e.activation(sq, ov, ACT.Square), t)
                t_o.append((h, ta, sq, ov))
        for i in range(2):
            sv = svt[:, i, :]
            V(lambda e, sv=sv: e.tensor_tensor(tmp[4], sv, sv, ALU.mult))
            ss = ctmp[:, 4 * i:4 * i + 4]
            t = V(lambda e, ss=ss: e.tensor_reduce(ss, tmp[4].rearrange("p (g c) -> p g c", g=4), AX, ALU.add))
            t = rstd(ss, ss, 128, t)
            sg = sv.rearrange("p (g c) -> p g c", g=4)
            t_sv = V(lambda e, sg=sg, ss=ss: e.tensor_tensor(sg, sg, ss.rearrange("p (g o) -> p g o", o=1).broadcast_to([128, 4, 128]),
                                                             ALU.mult), t)
        work.pop(0)()
        flush()
        for h, ta, sq, ov in t_o:
            b = 4 + h // 2
            tok = PE(lambda e, b=b, sq=sq: e.matmul(B[b][:, :], ones, sq, start=True, stop=True), ta, free[b])
            t = rstd(sq, B[b][:, :], 128, tok)
            free[b] = t
            V(lambda e, ov=ov, sq=sq: e.tensor_tensor(ov, ov, sq, ALU.mult), t)
            for j in (h - 1, h):
                t_oT = V(lambda e, j=j: e.scalar_tensor_tensor(oT[:, j, :], oT[:, j, :], vc_("hgn", j), gT[:, j, :], ALU.mult, ALU.mult))
        work.pop(0)()
        flush()

        for g in range(4):
            for i in range(2):
                o0 = 256 * (g % 2) + 128 * i
                tok = PE(lambda e, b=4 + g // 2, g=g, i=i, o0=o0: e.matmul(
                    B[b][:, o0:o0 + 128], svt[:, i, 128 * g:128 * g + 128], wst[:, g, :], start=True, stop=True),
                    t_sv, t_wst, free[4 + g // 2])
            if g % 2 == 0:
                continue
            for gg in (g - 1, g):
                pv = B[4 + g // 2][:, 256 * (gg % 2):256 * (gg % 2) + 256].rearrange("p (i t) -> p i t", i=2)
                bs = bsb[:, gg:gg + 1, :].broadcast_to([128, 2, 128])
                m = tmp[3][:, 0:256].rearrange("p (i t) -> p i t", i=2)
                t = V(lambda e, pv=pv, bs=bs, m=m, gg=gg: e.scalar_tensor_tensor(m, pv, vc_("sgn", gg), bs, ALU.mult, ALU.add),
                      tok, t_bsb)
                t_uT = V(lambda e, gg=gg: e.tensor_tensor(uT[:, gg, :], uT[:, gg, :], tmp[3][:, 0:256], ALU.mult))
            free[4 + g // 2] = t
        to = split_a(oTh, oTl, oT, t_oT)
        tu = split_a(uTh, uTl, uT, t_uT)
        while work:
            work.pop(0)()
            flush()
        t_hdone = PE.last()
        t_sab = [V.last(), A.last()]
        early_tok = [PE.last(), V.last(), A.last(), G.last()]



        t_mg = []
        for c in range(2):
            for which, (xh, xl, tx, Gt_) in enumerate(((oTh, oTl, to, SA), (uTh, uTl, tu, SB))):
                s = take()
                for half in range(2):
                    b = nextbank()
                    for j in range(2):
                        cs = slice(256 * half + 128 * j, 256 * half + 128 * j + 128)
                        tok = projT(s, cs, lambda k, xh=xh: xh[:, k, :], lambda k, xl=xl: xl[:, k, :], B[b][:, 256 * j:256 * j + 256],
                                    [free[b], tx], kn=4)
                    if half == 0:
                        ahead()
                    else:
                        done(s, tok)
                    k0 = 4 * c + 2 * half
                    gv = Gt_[:, k0:k0 + 2, :]
                    bv = B[b].rearrange("p (k t) -> p k t", k=2)
                    t = free[b] = V(lambda e, gv=gv, bv=bv: e.tensor_tensor(gv, gv, bv, ALU.mult), tok, t_sab)
                    if which:
                        mg = MG[:, k0:k0 + 2, :]
                        V(lambda e, mg=mg, gv=gv, k0=k0: e.tensor_tensor(mg, gv, SA[:, k0:k0 + 2, :], ALU.add), t_hdone)
                        t_mg += [split_a(MGh[:, k0:k0 + 2, :], MGl[:, k0:k0 + 2, :], mg, V.last())] * 2

        def wout(X, ah, al, wait, gate):
            xt = []
            for c in range(4):
                s = take()
                b = nextbank()
                for j in range(2):
                    tok = projT(s, slice(128 * j, 128 * j + 128), ah, al, B[b][:, 256 * j:256 * j + 256], [free[b]], per_k=wait)
                done(s, tok)
                ahead()
                for j in range(2):
                    db = 2 * c + j
                    ps = B[b][:, 256 * j:256 * j + 256]
                    if gate is not None:
                        tt = V(lambda e, db=db, ps=ps: e.scalar_tensor_tensor(X[:, db, :], ps, gate(db), X[:, db, :], ALU.mult, ALU.add), tok)
                    else:
                        tt = V(lambda e, db=db, ps=ps: e.tensor_tensor(X[:, db, :], ps, X[:, db, :], ALU.add), tok)
                free[b] = tt
                xt += [tt, tt]
            return xt

        t_x1 = wout(XX, lambda k: MGh[:, k, :], lambda k: MGl[:, k, :], t_mg, lambda db: mod[:, 16 + db, 0:1])
        late_tok = [PE.last(), V.last(), A.last()]

        z2 = [late]
        H2 = new(2048, z2).rearrange("p (k t) -> p k t", k=8)
        H2k = new(2048, z2).rearrange("p (i n) -> p i n", i=2)
        XS = new(4096, z2).rearrange("p (k n) -> p k n", k=8)
        Pm = new(1024, z2).rearrange("p (i e s) -> p i e s", i=2, e=16)
        PR = [new(256, z2).rearrange("p (i r s) -> p i r s", i=2, r=4) for _ in range(2)]
        MOE = new(2048, z2).rearrange("p (k t) -> p k t", k=8)
        Gt = [new(256, z2) for _ in range(2)]
        hid = [new(512, z2) for _ in range(2)]
        sgm = new(512, z2)
        hidT = [new(512, z2) for _ in range(2)]
        YE = [H2[:, 4 * i:4 * i + 4, :].rearrange("p k t -> p (k t)") for i in range(2)]
        af = new(256, z2)
        wk_ = new(256, z2)
        lgt = new(256, z2)
        m8 = new(32, z2)
        affk = new(32, z2).rearrange("p (i n) -> p i n", i=2)
        posk = new(32, z2).rearrange("p (i n) -> p i n", i=2)
        sm = new(64, z2)
        sq2 = MOE.rearrange("p k t -> p (k t)")
        rs2 = new(256, z2)

        def norm(X, dst, tx, scale, shift, SQb, rsb, bank, *w):
            sqv = SQb.rearrange("p (k t) -> p k t", k=8)
            for q in range(4):
                t = A(lambda e, q=q: e.activation(sqv[:, 2 * q:2 * q + 2, :], X[:, 2 * q:2 * q + 2, :], ACT.Square),
                      tx[2 * q + 1], *w)
                t = V(lambda e, q=q: e.tensor_tensor(sqv[:, 2 * q, :], sqv[:, 2 * q, :], sqv[:, 2 * q + 1, :], ALU.add), t)
                tok = PE(lambda e, q=q: e.matmul(B[bank][:, 0:256], ones, sqv[:, 2 * q, :], start=q == 0, stop=q == 3), t, free[bank])
            t = rstd(rsb, B[bank][:, 0:256], D, tok)
            free[bank] = t
            out_ = []
            for k in range(8):
                tv = V(lambda e, k=k: e.scalar_tensor_tensor(dst[:, k, :], X[:, k, :], scale(k), rsb, ALU.mult, ALU.mult), t)
                if shift is not None:
                    tv = A(lambda e, k=k: e.activation(dst[:, k, :], dst[:, k, :], ACT.Identity, bias=shift(k)), tv)
                out_.append(tv)
            return out_

        V(lambda e: e.scalar_tensor_tensor(swf, mod[:, 32:40, 0], 1.0, vc_("nffn", 0, 8), ALU.add, ALU.mult))
        t_h2 = norm(XX, H2, t_x1, lambda k: swf[:, k:k + 1], lambda k: mod[:, 24 + k, 0:1], sq2, rs2, 4, late_tok)

        for k in range(8):
            tok = PE(lambda e, k=k: e.matmul(B[5][0:16, 0:256], wr[:, k, :], H2[:, k, :], start=k == 0, stop=k == 7),
                     t_h2[k], t_wr, free[5])
        t = V(lambda e: e.tensor_copy(lgt[0:16, :], B[5][0:16, 0:256]), tok)
        free[5] = t
        for i in range(2):
            tok = PE(lambda e, i=i: e.transpose(B[6][:, 16 * i:16 * i + 16], lgt[0:16, 128 * i:128 * i + 128], ident[0:16, 0:16]), t, free[6])
        lp = B[6][:, 0:32].rearrange("p (i n) -> p i n", i=2)
        bc = lambda x: x.rearrange("p (i o) -> p i o", o=1).broadcast_to([128, 2, 16])
        V(lambda e: e.tensor_reduce(sm[:, 0:2], lp, AX, ALU.max), tok)
        t = V(lambda e: e.tensor_tensor(affk, lp, bc(sm[:, 0:2]), ALU.subtract))
        free[6] = t
        t = A(lambda e: e.activation(affk, affk, ACT.Exp), t)
        V(lambda e: e.tensor_reduce(sm[:, 2:4], affk, AX, ALU.add), t)
        V(lambda e: e.reciprocal(sm[:, 4:6], sm[:, 2:4]))
        t_aff = V(lambda e: e.tensor_tensor(affk, affk, bc(sm[:, 4:6]), ALU.mult))
        for i in range(2):
            tok = PE(lambda e, i=i: e.transpose(B[6][0:16, 128 * i:128 * i + 128], affk[:, i, :], ident), t_aff, free[6])
        for i in range(2):
            for c in range(2):
                b = (0, 1, 2, 3)[2 * i + c]
                for j in range(4):
                    k = 4 * c + j
                    tk2 = PE(lambda e, b=b, i=i, j=j, k=k: e.transpose(B[b][:, 128 * j:128 * j + 128], H2[:, k, 128 * i:128 * i + 128], ident),
                             t_h2[-1], free[b])
                t_h2k = A(lambda e, b=b, i=i, c=c: e.activation(H2k[:, i, 512 * c:512 * c + 512], B[b][:, :], ACT.Copy), tk2)
                free[b] = t_h2k
        w16 = wk_[0:16, :]
        t = V(lambda e: e.tensor_copy(w16, B[6][0:16, 0:256]), tok)
        free[6] = t
        for r in range(4):
            V(lambda e, r=r: e.max(m8[0:16, 8 * r:8 * r + 8], w16))
            V(lambda e, r=r: e.match_replace(w16, m8[0:16, 8 * r:8 * r + 8], w16, -1.0))
        V(lambda e: e.tensor_scalar(w16, w16, 0.0, None, ALU.is_lt))
        V(lambda e: e.tensor_tensor_scan(af[0:16, :], ones[0:16, 0:1].broadcast_to([16, 256]), w16, 0.0, ALU.mult, ALU.add))
        t = V(lambda e: e.tensor_tensor(af[0:16, :], af[0:16, :], w16, ALU.mult))
        for i in range(2):
            tok = PE(lambda e, i=i: e.transpose(B[6][:, 16 * i:16 * i + 16], af[0:16, 128 * i:128 * i + 128], ident[0:16, 0:16]), t, free[6])
        t = V(lambda e: e.tensor_copy(posk, lp), tok)
        free[6] = t
        io = iot.rearrange("p (o s) -> p o s", o=1).broadcast_to([128, 16, 32])
        for i in range(2):
            t_P = V(lambda e, i=i: e.tensor_tensor(Pm[:, i, :, :], io, posk[:, i, :].rearrange("p (n o) -> p n o", o=1)
                                                   .broadcast_to([128, 16, 32]), ALU.is_equal), t_iot)
        t_xs = {}

        def gather(half, k):
            b = 6 + k % 2
            for i in range(2):
                tok = PE(lambda e, i=i: e.matmul(B[b][:, 0:256], H2k[:, i, 128 * k:128 * k + 128],
                                                 Pm[:, i, 8 * half:8 * half + 8, :], start=i == 0, stop=i == 1),
                         t_P, t_h2k, free[b])
            free[b] = A(lambda e: e.activation(XS[:, k, 256 * half:256 * half + 256], B[b][:, 0:256], ACT.Copy), tok)
            t_xs[half, k] = free[b]

        gather(0, 0)
        gather(0, 1)

        for i in range(MORE_SLOTS):
            s = Slot()
            s.free = early_tok if i < EARLY else late_tok
            last_done[BASE_SLOTS + i] = s
        nx = at[0] % BASE_SLOTS
        more_ = [BASE_SLOTS + i for i in range(MORE_SLOTS)]
        ring[:] = more_[:EARLY] + ring[nx:] + ring[:nx] + more_[EARLY:]
        at[0] = 0
        wg, wu = a["wg"], a["wu"]
        wd = a["wd"].rearrange("e (j c p) n -> e c p j n", j=4, c=4)
        GB, UB, TB, D0, D1, S0, S1 = 0, 1, 2, 3, 4, 5, 6
        y_tok = {}
        g_tok, pe_sc, hid_pe, h2_pe, g_pe = {}, {}, {}, {}, {}

        def prep_g(e_):
            pr = PR[e_ % 2]
            tp = G(lambda e: e.tensor_tensor(pr, Pm[:, :, e_:e_ + 1, :].broadcast_to([128, 2, 4, 32]),
                                             affk[:, :, e_:e_ + 1].rearrange("p i (n o) -> p i n o", o=1).broadcast_to([128, 2, 4, 32]),
                                             ALU.mult), t_P, g_pe.get(e_ - 2))
            for i in range(2):
                tok = PE(lambda e, i=i: e.transpose(B[7][:, 128 * i:128 * i + 128], pr[:, i, :, :].rearrange("p r s -> p (r s)"), ident),
                         tp, free[7])
            g_pe[e_] = tok
            g_tok[e_] = A(lambda e: e.activation(Gt[e_ % 2], B[7][:, 0:256], ACT.Copy), tok, pe_sc.get(e_ - 2))
            free[7] = g_tok[e_]

        def scatter(e_):
            for q in range(4):
                b = (S0, S1)[q % 2]
                for j in range(2):
                    db = 2 * q + j
                    tok = PE(lambda e, b=b, j=j, db=db: e.matmul(B[b][:, 256 * j:256 * j + 256], YE[e_ % 2][:, 128 * db:128 * db + 128],
                                                                 Gt[e_ % 2], start=True, stop=True),
                             y_tok[e_], g_tok[e_], free[b])
                mv = MOE[:, 2 * q:2 * q + 2, :].rearrange("p k t -> p (k t)")
                if e_ == 0:
                    free[b] = V(lambda e, b=b, mv=mv: e.tensor_copy(mv, B[b][:, :]), tok)
                else:
                    free[b] = V(lambda e, b=b, mv=mv: e.tensor_tensor(mv, mv, B[b][:, :], ALU.add), tok)
            pe_sc[e_] = tok

        def up(src, e_, bank, hook=None):
            for k in range(8):
                s = stream(src[e_, k * 128:(k + 1) * 128, :], [2048])
                if (0, k + 2) not in t_xs and k < 6:
                    gather(0, k + 2)
                for j in range(4):
                    tok = PE(lambda e, k=k, j=j, s=s: e.matmul(B[bank][32 * j:32 * j + 32, :], XS[:, k, 32 * e_:32 * e_ + 32],
                                                               s.v[:, 512 * j:512 * j + 512], start=k == 0, stop=k == 7),
                             s.t, t_xs[e_ // 8, k], free[bank])
                done(s, tok)
                if hook and k == 3:
                    hook()
            return tok

        for e_ in range(NE):
            tg = up(wg, e_, GB, (lambda: scatter(e_ - 1)) if e_ else None)
            if e_ == 0:
                for k in range(8):
                    gather(1, k)
            prep_g(e_)
            t, _ = sigmoid(sgm, B[GB][:, :], tg)
            hd, hT_ = hid[e_ % 2], hidT[e_ % 2]
            free[GB] = V(lambda e: e.tensor_tensor(sgm, sgm, B[GB][:, :], ALU.mult), t)
            tu = up(wu, e_, UB)
            t = V(lambda e, hd=hd: e.tensor_tensor(hd, sgm, B[UB][:, :], ALU.mult), tu, hid_pe.get(e_ - 2))
            free[UB] = t
            for c in range(4):
                tok = PE(lambda e, c=c, hd=hd: e.transpose(B[TB][:, 128 * c:128 * c + 128], hd[:, 128 * c:128 * c + 128], ident), t, free[TB])
            hid_pe[e_] = tok
            th = A(lambda e, hT_=hT_: e.activation(hT_, B[TB][:, :], ACT.Copy), tok, h2_pe.get(e_ - 2))
            free[TB] = th
            for c in range(4):
                ss = [stream(wd[e_, c, :, 2 * jj:2 * jj + 2, :], [2, 1024]) for jj in range(2)]
                for db in range(2):
                    for j in range(4):
                        tok = PE(lambda e, c=c, j=j, db=db, s=ss[j // 2], hT_=hT_: e.matmul(
                            B[(D0, D1)[db]][32 * j:32 * j + 32, :], hT_[:, 128 * c + 32 * j:128 * c + 32 * j + 32],
                            s.v[:, j % 2, 512 * db:512 * db + 512], start=c == 0, stop=c == 3),
                            ss[j // 2].t, th, free[D0], free[D1])
                for s in ss:
                    done(s, tok)
            h2_pe[e_] = tok
            ye = YE[e_ % 2]
            free[D0] = A(lambda e, ye=ye: e.activation(ye[:, 0:512], B[D0][:, :], ACT.Copy), tok, pe_sc.get(e_ - 2))
            free[D1] = V(lambda e, ye=ye: e.tensor_copy(ye[:, 512:1024], B[D1][:, :]), tok, pe_sc.get(e_ - 2))
            y_tok[e_] = [free[D0], free[D1]]
        scatter(NE - 1)
        t_x2 = [V(lambda e, k=k: e.scalar_tensor_tensor(XX[:, k, :], MOE[:, k, :], mod[:, 40 + k, 0:1], XX[:, k, :], ALU.mult, ALU.add))
                for k in range(8)]

        z3 = [zone]
        v8 = lambda x: x.rearrange("p (k t) -> p k t", k=8)
        HN0, C20, o20, PT2 = (new(2048, z3) for _ in range(4))
        HNh = v8(R(new(2048, z3), 2048))
        C2h = v8(R(new(2048, z3), 2048))
        WH2 = [R(new(2048, z3), 2048) for _ in range(3)]
        UU0 = new(8 * 258, z3)
        UU = UU0.rearrange("p (k t) -> p k t", k=8)
        SQ3 = new(2048, z3)
        GA = v8(SQ3)
        GC = v8(new(2048, z3))
        vk0 = new(2048, z3)
        vk = vk0.rearrange("p (i n) -> p i n", i=2)
        qq = new(2048, z3)
        q2 = qq[:, 0:1024].rearrange("p (h t) -> p h t", h=4)
        k2 = qq[:, 1024:2048].rearrange("p (h t) -> p h t", h=4)
        b2 = new(1024, z3).rearrange("p (h t) -> p h t", h=4)
        E20 = new(2048, z3)
        E2 = [E20[:, 1024 * i:1024 * i + 1024].rearrange("p (h t) -> p h t", h=4) for i in range(2)]
        M2 = [new(1024, z3).rearrange("p (h t) -> p h t", h=4) for _ in range(2)]
        tp2 = [new(512, z3) for _ in range(6)]
        gkl = new(256, z3)
        rs3 = new(256, z3)
        HN, C2, o2, MG2 = v8(HN0), v8(C20), v8(o20), v8(PT2)
        HNl, C2l, o2l, MGl2, o2h, MGh2 = (v8(R(x, 2048)) for x in (HN0, C20, o20, PT2, E20, UU0))
        PTv = PT2.rearrange("p (j h i) -> p j h i", j=2, h=4)
        w2 = a["w_in2"].rearrange("(k p) n -> p k n", p=128)
        CC, XO, CB, ZC, ZO, GAO, GCO = 4112, 5136, 3088, 6160, 2048, 7184, 8208
        wants(w2, 3072, 16)
        for off, n in ((0, 2), (512, 2), (1024, 4), (CC, 4), (XO, 4), (CB, 4), (ZC, 4), (ZO, 4), (GAO, 4), (GCO, 4)):
            for hh in range(n):
                wants(w2, off + 256 * hh)
        wa2 = a["wa2"].rearrange("(k p) n -> p k n", p=128)
        wc2 = a["wc2"].rearrange("(k p) n -> p k n", p=128)
        for c in range(4):
            wants(wa2, 256 * c)
            wants(wc2, 256 * c)
        for name in ("wo2", "wpg"):
            for c in range(4):
                wants(a[name].rearrange("(k p) n -> p k n", p=128), 256 * c)
        ring[:] = ring[at[0] % len(ring):] + ring[:at[0] % len(ring)]
        ring[:] = [i for i in ring if i < BASE_SLOTS]
        at[0] = 0
        quiet = [PE.last(), V.last(), A.last(), G.last()]
        whs[0] = WH2
        wh_free[:] = [quiet] * 3

        sa3, sb3 = (x.rearrange("p (k t) -> p k t", k=8) for x in (SQ3, vk0))
        V(lambda e: e.tensor_tensor(swf, vc_("fnw", 0, 8), vc_("nm2", 0, 8), ALU.mult))
        ahead()
        for q in range(4):
            xq = XX[:, 2 * q:2 * q + 2, :]
            t0 = V(lambda e, q=q, xq=xq: e.tensor_tensor(sa3[:, 2 * q:2 * q + 2, :], xq, xq, ALU.mult), quiet)
            for k in (2 * q, 2 * q + 1):
                t1 = A(lambda e, k=k: e.activation(sb3[:, k, :], XX[:, k, :], ACT.Square, scale=vc_("fnw", k)), t_x2[k], quiet)
            t0, t1 = (f(lambda e, q=q, x=x: e.tensor_tensor(x[:, 2 * q, :], x[:, 2 * q, :], x[:, 2 * q + 1, :], ALU.add), y)
                      for f, x, y in ((V, sa3, t0), (G, sb3, t1)))
            PE(lambda e, q=q: e.matmul(B[4][:, 0:256], ones, sa3[:, 2 * q, :], start=q == 0, stop=q == 3), t0, free[4])
            tok = PE(lambda e, q=q: e.matmul(B[5][:, 0:256], ones, sb3[:, 2 * q, :], start=q == 0, stop=q == 3), t1, free[5])
        r1, r2 = rs3, gkl
        t = free[4] = rstd(r1, B[4][:, 0:256], D, tok)
        ahead()
        V(lambda e: e.tensor_tensor(r2, r1, r1, ALU.mult), t)
        t = free[5] = V(lambda e: e.tensor_tensor(r2, r2, B[5][:, 0:256], ALU.mult), tok)
        t = rstd(r2, r2, D, t)
        t = V(lambda e: e.tensor_tensor(r2, r1, r2, ALU.mult), t)
        t_n = [V(lambda e, k=k: e.scalar_tensor_tensor(HN[:, k, :], XX[:, k, :], swf[:, k:k + 1], r2, ALU.mult, ALU.mult), t)
               for k in range(8)]

        def split_h(t):
            return [split_a(HNh[:, k, :], HNl[:, k, :], HN[:, k, :], t[k]) for k in range(8)]

        t_hn = split_h(t_n)
        ahead()
        for k in range(8):
            V(lambda e, k=k: e.scalar_tensor_tensor(XX[:, k, :], XX[:, k, :], vc_("fnw", k), r1, ALU.mult, ALU.mult))
        V(lambda e: e.memset(UU[:, :, 0:2], 0.0))
        z_pt = V(lambda e: e.memset(PT2, 0.0))
        Hn = (lambda k: HNh[:, k, :], lambda k: HNl[:, k, :])

        s = take()
        tok = projT(s, slice(0, 16), *Hn, B[4][0:16, 0:256], [free[4]], per_k=t_hn)
        done(s, tok)
        t = free[4] = V(lambda e: e.tensor_copy(gkl[0:16, :], B[4][0:16, 0:256]), tok)
        sgk = stream(a["w_gk2"], [512], parts=16)
        onr = ones[:, 0:1].broadcast_to([128, 256])

        def gate():
            nonlocal t_b2
            for h in range(4):
                tok = PE(lambda e, h=h: e.matmul(B[h // 2][:, 256 * (h % 2):256 * (h % 2) + 256], sgk.v[:, 128 * h:128 * h + 128],
                                                 gkl[0:16, :], start=True, stop=True), sgk.t, t_gk, free[0], free[1])
            done(sgk, tok)
            for u in range(2):
                zz, aa = tp2[2 * u], tp2[2 * u + 1]
                for j in range(2):
                    t = V(lambda e, j=j, u=u, zz=zz: e.tensor_scalar(zz[:, 256 * j:256 * j + 256], B[u][:, 256 * j:256 * j + 256],
                                                                    vc_("bgk", 2 * u + j), None, ALU.add), tok)
                free[u] = t
                t = V(lambda e, zz=zz, aa=aa: e.scalar_tensor_tensor(aa, zz, -1.0, zz, ALU.mult, ALU.max))
                A(lambda e, aa=aa: e.activation(aa, aa, ACT.Exp, scale=-1.0), t)
                t = A(lambda e, aa=aa: e.activation(aa, aa, ACT.Ln, bias=ones[:, 0:1]))
                V(lambda e, zz=zz, aa=aa: e.scalar_tensor_tensor(aa, zz, 0.0, aa, ALU.min, ALU.subtract), t)
                for j in range(2):
                    t_b2 = V(lambda e, aa=aa, u=u, j=j: e.tensor_tensor_scan(b2[:, 2 * u + j, :], onr, aa[:, 256 * j:256 * j + 256],
                                                                            0.0, ALU.mult, ALU.add))

        t_b2, t_gk = None, t

        def p2(hh, fn):
            s = take()
            b = nextbank()
            for j in range(2):
                tok = projT(s, slice(128 * j, 128 * j + 128), *Hn, B[b][:, 256 * j:256 * j + 256], [free[b]])
            done(s, tok)
            ahead()
            flush()
            r = fn(hh, B[b][:, :], tok, b)
            if r is not None:
                free[b] = r

        pair = lambda x, hh: x[:, 2 * hh:2 * hh + 2, :].rearrange("p h t -> p (h t)")
        t_qk = []

        def e_q(dst, scale):
            def f(hh, ps, tok, b):
                t_qk.append(A(lambda e: e.activation(pair(dst, hh), ps, ACT.Copy, scale=scale), tok))
                return t_qk[-1]
            return f

        p2(0, e_q(q2, 128 ** -0.5))
        gate()
        p2(1, e_q(q2, 128 ** -0.5))
        p2(0, e_q(k2, 1.0))
        p2(1, e_q(k2, 1.0))
        t_v2 = []

        def p_v2(hh):
            s = take()
            for i in range(2):
                b = nextbank()
                ts_ = slice(128 * i, 128 * i + 128)
                tok = mm3(B[b][:, 0:256], lambda k: s.h[:, k, :], lambda k: s.l[:, k, :], lambda k, ts_=ts_: HNh[:, k, ts_],
                          lambda k, ts_=ts_: HNl[:, k, ts_], 8, [s.t, free[b]], w_first=False)
                free[b] = A(lambda e, b=b, i=i, hh=hh: e.activation(vk[:, i, 256 * hh:256 * hh + 256], B[b][:, 0:256], ACT.Copy), tok)
            done(s, tok)
            ahead()
            t_v2.append(free[b])

        K_, Q_ = E2
        MK_, MQ_ = M2
        I16 = 1.0 / 16.0
        last_mm = [None]

        def elements2(s_):
            n = 1024 // (2 * s_)
            bv = split(b2, s_)
            Kv, Qv = split(K_, s_), split(Q_, s_)
            r = bv[:, :, 0, s_ - 1:s_].broadcast_to([128, n, s_])
            V(lambda e: e.tensor_tensor(Kv[:, :, 0, :], r, bv[:, :, 0, :], ALU.subtract))
            t = V(lambda e: e.tensor_tensor(Qv[:, :, 1, :], bv[:, :, 1, :], r, ALU.subtract))
            A(lambda e: e.activation(Kv[:, :, 0, :], Kv[:, :, 0, :], ACT.Exp, scale=I16), t)
            t = A(lambda e: e.activation(Qv[:, :, 1, :], Qv[:, :, 1, :], ACT.Exp, scale=I16))
            V(lambda e: e.tensor_tensor(split(MK_, s_)[:, :, 0, :], split(k2, s_)[:, :, 0, :], Kv[:, :, 0, :], ALU.mult),
              t, t_qk, last_mm[0])
            return V(lambda e: e.tensor_tensor(split(MQ_, s_)[:, :, 1, :], split(q2, s_)[:, :, 1, :], Qv[:, :, 1, :], ALU.mult))

        def scores2(s_, t):
            for j in range(1 if s_ == 128 else 2):
                for h in range(4):
                    if s_ == 128:
                        o_, lh, rh = B[4][:, 128 * h:128 * h + 128], MK_[:, h, 0:128], MQ_[:, h, 128:256]
                    else:
                        c0 = 256 * j + 64 * h
                        o_, lh, rh = B[5][0:64, c0:c0 + 64], MK_[:, h, 128 * j:128 * j + 64], MQ_[:, h, 128 * j + 64:128 * j + 128]
                    tok = PE(lambda e, o_=o_, lh=lh, rh=rh: e.matmul(o_, lh, rh, start=True, stop=True), t, free[4], free[5])
            last_mm[0] = tok
            if s_ == 128:
                free[4] = V(lambda e: e.tensor_copy(PTv[:, 0, :, 128:256], B[4].rearrange("p (h i) -> p h i", h=4)), tok, z_pt)
            else:
                for j in range(2):
                    free[5] = V(lambda e, j=j: e.tensor_copy(PTv[0:64, j, :, 128 * j + 64:128 * j + 128],
                                                             B[5][0:64, 256 * j:256 * j + 256].rearrange("p (h i) -> p h i", h=4)), tok)

        p_v2(0)
        t = elements2(128)
        p_v2(1)
        scores2(128, t)
        t = elements2(64)
        p_v2(2)
        scores2(64, t)
        bc4 = b2.rearrange("p h (n t) -> p h n t", n=4)
        K4 = K_.rearrange("p h (n t) -> p h n t", n=4)
        V(lambda e: e.tensor_copy(K4[:, :, 0, :], bc4[:, :, 0, :]))
        t = V(lambda e: e.tensor_tensor(K4[:, :, 1:4, :], bc4[:, :, 1:4, :], bc4[:, :, 0:3, 63:64].broadcast_to([128, 4, 3, 64]), ALU.subtract))
        A(lambda e: e.activation(Q_, K_, ACT.Exp, scale=I16), t)
        t = A(lambda e: e.activation(K_, K_, ACT.Exp, scale=-I16))
        V(lambda e: e.tensor_tensor(MK_, k2, K_, ALU.mult), t, last_mm[0])
        t = V(lambda e: e.tensor_tensor(MQ_, q2, Q_, ALU.mult))
        p_v2(3)
        e_cc = lambda hh, ps, tok, b: A(lambda e: e.activation(pair(C2, hh), ps, ACT.Copy), tok)
        p2(0, e_cc)
        for j in range(2):
            for h in range(4):
                tok = PE(lambda e, j=j, h=h: e.matmul(B[4 + j][:, 128 * h:128 * h + 128], MK_[:, h, 128 * j:128 * j + 128],
                                                      MQ_[:, h, 128 * j:128 * j + 128], start=True, stop=True), t, free[4], free[5])
            lm = msk[:, 8, :].rearrange("p (o i) -> p o i", o=1).broadcast_to([128, 4, 128])
            t_pt2 = V(lambda e, j=j, lm=lm: e.copy_predicated(PTv[:, j, :, 128 * j:128 * j + 128], lm,
                                                              B[4 + j].rearrange("p (h i) -> p h i", h=4)), tok)
            free[4 + j] = t_pt2
        t_scores = [PE.last(), V.last(), A.last()]
        for hh in range(1, 4):
            p2(hh, e_cc)
        t_cc = A.last()

        def attend(h):
            b = 4 + h % 2
            for w in range(2):
                ps = B[b][:, 256 * w:256 * w + 256]
                vs = slice(256 * h + 128 * w, 256 * h + 128 * w + 128)
                PE(lambda e, ps=ps, vs=vs: e.matmul(ps, vk[:, 0, vs], PTv[:, 0, h, :], start=True, stop=False), t_pt2, t_v2, free[b])
                tok = PE(lambda e, ps=ps, vs=vs: e.matmul(ps[:, 128:256], vk[:, 1, vs], PTv[:, 1, h, 128:256], start=False, stop=True))
            ov = pair(o2, h)
            t = free[b] = V(lambda e: e.tensor_copy(ov, B[b]), tok)
            t_sq.append(A(lambda e: e.activation(tp2[2 + h], ov, ACT.Square), t))

        def attend_norm(u):
            for h in (2 * u, 2 * u + 1):
                for w in range(2):
                    tok = PE(lambda e, h=h, w=w: e.matmul(B[4 + u][:, 256 * (h % 2):256 * (h % 2) + 256], ones,
                                                          tp2[2 + h][:, 256 * w:256 * w + 256], start=w == 0, stop=w == 1),
                             t_sq[h], free[4 + u])
            r = tp2[2 + 2 * u]
            t = free[4 + u] = rstd(r, B[4 + u], 256, tok)
            for h in (2 * u, 2 * u + 1):
                rv = r[:, 256 * (h % 2):256 * (h % 2) + 256]
                for w in range(2):
                    V(lambda e, h=h, w=w, rv=rv: e.scalar_tensor_tensor(o2[:, 2 * h + w, :], o2[:, 2 * h + w, :], vc_("gng", w), rv,
                                                                        ALU.mult, ALU.mult), t)

        t_sq = []

        def e_x(hh, ps, tok, b):
            u = UU[:, 2 * hh:2 * hh + 2, 2:258]
            r = V(lambda e: e.tensor_tensor(u, C2[:, 2 * hh:2 * hh + 2, :], ps.rearrange("p (h t) -> p h t", h=2), ALU.mult), tok, t_cc)
            for k in (2 * hh, 2 * hh + 1):
                V(lambda e, k=k: e.tensor_scalar(C2[:, k, :], UU[:, k, 2:258], vc_("cw", 16 + k), None, ALU.mult))
                for w in (1, 0):
                    V(lambda e, k=k, w=w: e.scalar_tensor_tensor(C2[:, k, :], UU[:, k, w:w + 256], vc_("cw", 8 * w + k), C2[:, k, :],
                                                                 ALU.mult, ALU.add))
            return r

        for hh in range(4):
            p2(hh, e_x)
            attend(hh)
        t_att = PE.last()
        for hh in range(4):
            p2(hh, lambda hh, ps, tok, b: V(lambda e: e.tensor_tensor(pair(C2, hh), pair(C2, hh), ps, ALU.mult), tok))
            if hh < 2:
                attend_norm(hh)

        def e_silu(into, hi, lo, toks):
            def f(hh, ps, tok, b):
                dst, x = tp2[hh % 2], pair(into, hh)
                t, _ = sigmoid(dst, ps, tok)

                def rest_():
                    r = V(lambda e: e.tensor_tensor(dst, dst, ps, ALU.mult), t)
                    m = V(lambda e: e.tensor_tensor(x, x, dst, ALU.mult))
                    h_ = A(lambda e: e.activation(pair(hi, hh), x, ACT.Copy), m, t_scores)
                    toks.append(G(lambda e: e.tensor_tensor(pair(lo, hh), x, pair(hi, hh).bitcast(F32), ALU.subtract), h_))
                    return r
                defer(b, rest_)
            return f

        t_c2, t_o2 = [], []
        for hh in range(4):
            p2(hh, e_silu(C2, C2h, C2l, t_c2))
        for hh in range(4):
            p2(hh, e_silu(o2, o2h, o2l, t_o2))

        def e_gate(buf, off):
            def f(hh, ps, tok, b):
                for j in range(2):
                    k = 2 * hh + j
                    w = V(lambda e, j=j, k=k: e.tensor_scalar(buf[:, k, :], ps[:, 256 * j:256 * j + 256], vc_("bm2", off + k), -43.0,
                                                              ALU.add, ALU.max), tok)
                pv = pair(buf, hh)
                A(lambda e: e.activation(pv, pv, ACT.Exp, scale=-1.0), w)
                A(lambda e: e.activation(pv, pv, ACT.Ln, bias=ones[:, 0:1]))
                A(lambda e: e.activation(pv, pv, ACT.Exp, scale=-1.0))
                return w
            return f

        for hh in range(4):
            p2(hh, e_gate(GA, 0))
        for i, x in enumerate((vk0, qq)):
            s = Slot()
            s.free = [t_scores, t_att]
            last_done[BASE_SLOTS + MORE_SLOTS + i] = s
            allslots[BASE_SLOTS + MORE_SLOTS + i] = x
        sw = stream(a["wpp"].rearrange("(k p) n -> p k n", p=128), [2, 1024], i=BASE_SLOTS + MORE_SLOTS)
        sp = stream(a["pT"].rearrange("(k p) t -> p k t", p=128), [2, 256], i=BASE_SLOTS + MORE_SLOTS + 1)
        for hh in range(4):
            p2(hh, e_gate(GC, 8))
        t_gg = A.last()
        t_pt_read = PE.last()
        t_mg = []
        for c in range(4):
            for half, (xh, xl, tx, gx) in enumerate(((o2h, o2l, t_o2, GA), (C2h, C2l, t_c2, GC))):
                s = take()
                b = nextbank()
                for j in range(2):
                    tok = projT(s, slice(128 * j, 128 * j + 128), lambda k, xh=xh: xh[:, k, :], lambda k, xl=xl: xl[:, k, :],
                                B[b][:, 256 * j:256 * j + 256], [free[b], tx])
                done(s, tok)
                ahead()
                free[b] = V(lambda e, b=b, c=c, gx=gx, half=half: e.tensor_tensor(tp2[4 + half], pair(gx, c), B[b], ALU.mult), tok, t_gg)
            t = V(lambda e, c=c: e.tensor_tensor(pair(MG2, c), tp2[4], tp2[5], ALU.add), t_pt_read)
            t_mg += [split_a(pair(MGh2, c), pair(MGl2, c), pair(MG2, c), t)] * 2
        t = wout(XX, lambda k: MGh2[:, k, :], lambda k: MGl2[:, k, :], t_mg, None)
        for db in range(8):
            b = (4, 5, 0, 1)[db // 2]
            for k in range(2):
                tok = PE(lambda e, db=db, b=b, k=k: e.matmul(B[b][:, 256 * (db % 2):256 * (db % 2) + 256], sw.v[:, k, 128 * db:128 * db + 128],
                                                             sp.v[:, k, :], start=k == 0, stop=k == 1), sw.t, sp.t, free[b])
        t_pp = tok
        t = norm(XX, HN, t, lambda k: vc_("nple", k), None, SQ3, rs3, 6, PE.last())
        t_h3 = split_h(t)
        t_x3 = {}
        for c in range(4):
            s = take()
            b1 = nextbank()
            for j in range(2):
                tok = projT(s, slice(128 * j, 128 * j + 128), *Hn, B[b1][:, 256 * j:256 * j + 256], [free[b1]], per_k=t_h3)
            done(s, tok)
            ahead()
            flush()
            sg, pb = tp2[c % 2], B[(4, 5, 0, 1)[c]]
            t, free[b1] = sigmoid(sg, B[b1], tok)

            def gated(sg=sg, pb=pb, c=c, t=t):
                V(lambda e: e.tensor_tensor(sg, sg, pb, ALU.mult), t, t_pp)
                t_x3[2 * c + 1] = V(lambda e: e.tensor_tensor(pair(XX, c), pair(XX, c), sg, ALU.add))
                return t_x3[2 * c + 1]
            defer(4 + c % 2, gated)
        flush()
        FINAL = MG2
        t = norm(XX, MG2, t_x3, lambda k: vc_("nfin", k), None, SQ3, rs3, 6, PE.last())

        finish(FINAL, t)


def pack(inp):
    f = lambda x: np.ascontiguousarray(np.asarray(x)).astype(np.float32, copy=False)
    col = lambda x: np.asarray(x).reshape(-1, 128).T
    c2 = np.stack([np.asarray(inp["c"]).reshape(8, 128), np.asarray(inp["c_ctx"]).reshape(8, 128)], 1)
    parts = [c2.reshape(16, 128).T, col(inp["ada_b"]), col(inp["norm_mix_w"]), col(inp["norm_ffn_w"]),
             col(inp["hgrn_lb_logits"]), col(inp["hgrn_norm_w"]), col(inp["sgu_norm_w"]), col(inp["final_norm_w"]),
             col(inp["norm_mix_g_2"]), col(inp["b_merge_2"]), col(inp["b_gk_2"]), col(inp["gla_norm_g_2"]),
             col(inp["conv_w_2"]), col(inp["norm_ple_g_2"]), col(inp["norm_final_g_2"]),
             np.full((128, 1), EPS, np.float32)]
    vec = np.concatenate(parts, 1)
    assert vec.shape == (128, VN)
    i = np.arange(128)
    masks = np.stack([(i[:, None] // (2 * s) == i[None, :] // (2 * s)) for s in (64, 64, 32, 16, 8, 4, 2, 1)], 1)
    leaf = (i[:, None] // 64 == i[None, :] // 64) & (i[:, None] <= i[None, :])
    masks = np.concatenate([masks[:, 1:], np.eye(128, dtype=bool)[:, None, :], leaf[:, None, :]], 1).astype(np.float32)
    return dict(
        vec=f(vec), msk=np.ascontiguousarray(masks.reshape(128, 1152)), ident=np.eye(128, dtype=np.float32),
        iota=np.tile(np.arange(1, 33, dtype=np.float32), (128, 1)),
        x=f(inp["x"][0].T), ctx=f(inp["ctx"][0].T), ada_w=f(inp["ada_w"][0]), w_in=f(inp["w_in"][0]),
        wst=f(np.asarray(inp["sgu_w"])[0].transpose(0, 2, 1)), sgu_b=f(inp["sgu_b"][0]),
        w_branch_a=f(inp["w_branch_a"][0]), w_branch_b=f(inp["w_branch_b"][0]), w_out=f(inp["w_out"][0]),
        router_w=f(inp["router_w"][0]), wg=f(inp["expert_w_gate"][0]), wu=f(inp["expert_w_up"][0]),
        wd=f(inp["expert_w_down"][0]),
        w_in2=f(inp["w_in_2"][0]), w_gk2=f(inp["w_gk2_2"][0]), wa2=f(inp["w_branch_a_2"][0]),
        wc2=f(inp["w_branch_c_2"][0]), wo2=f(inp["w_out_2"][0]), wpg=f(inp["w_ple_gate_2"][0]),
        wpp=f(inp["w_ple_proj_2"][0]), pT=f(np.asarray(inp["p_2"])[0, 0].T),
    )


def kernel(**inputs):
    import concourse.bacc as _bacc
    from concourse.bass_utils import run_bass_kernel_spmd as _run

    nc = _bacc.Bacc("TRN2", target_bir_lowering=False, num_devices=1)
    arrays = {f"in_{k}": v for k, v in pack(inputs).items()}
    aps = {k[3:]: nc.dram_tensor(k, v.shape, mybir.dt.from_np(v.dtype), kind="ExternalInput").ap() for k, v in arrays.items()}
    out = nc.dram_tensor("out_dram", (D, T), F32, kind="ExternalOutput").ap()
    program(nc, aps, out)
    r = _run(nc, [arrays], core_ids=[0])
    return np.ascontiguousarray(r.results[0]["out_dram"].T).reshape(1, T, D)
```
